# Optimizing a Trainium2 kernel written in Bass

```python
import math
import jax
import jax.numpy as jnp
from jax import lax
import numpy as np

D_MODEL = 1024
BATCH = 1
SEQ = 512
DEPTH = 2

N_MIXERS = 2
N_LAYERS_A = (DEPTH + 1) // 2
N_LAYERS_B = DEPTH // 2
PLE_DIM = 256
NORM_EPS = 1e-6

SSD_D_INNER = 2 * D_MODEL
SSD_HEADDIM = 64
SSD_HEADS = SSD_D_INNER // SSD_HEADDIM
SSD_GROUPS = 4
SSD_HPG = SSD_HEADS // SSD_GROUPS
SSD_STATE = 128
SSD_CONV = 5
SSD_CHUNK = 128
SSD_BC_DIM = SSD_GROUPS * SSD_STATE
SSD_CONV_DIM = SSD_D_INNER + 2 * SSD_BC_DIM
SSD_IN_DIM = SSD_D_INNER + SSD_CONV_DIM + 2 * SSD_HEADS
SSD_DT_MIN = 1e-3
SSD_DT_MAX = 1e-1

S5_GROUP = 16
S5_GROUPS = D_MODEL // S5_GROUP
S5_STATE = 64
S5_STEP_MIN = 1e-3
S5_STEP_MAX = 1e-1

FFN_HIDDEN = 2816
FFN_CONV = 3

kernel_name = 'bidir_hybrid_ssd_s5_convffn'

def rmsnorm(x, w):
    xf = x.astype(jnp.float32)
    xf = xf * lax.rsqrt(jnp.mean(xf * xf, axis=-1, keepdims=True) + NORM_EPS)
    return (xf * w.astype(jnp.float32)).astype(x.dtype)

def dwconv_centred(u, w, b):
    k = w.shape[0]
    half = k // 2
    seq = u.shape[1]
    upad = jnp.pad(u, ((0, 0), (half, half), (0, 0)))
    out = b + upad[:, 0:seq] * w[0]
    for t in range(1, k):
        out = out + upad[:, t:t + seq] * w[t]
    return out

def segsum(a):
    cs = jnp.cumsum(a, axis=-1)
    t = a.shape[-1]
    diff = cs[..., :, None] - cs[..., None, :]
    mask = jnp.tril(jnp.ones((t, t), dtype=bool))
    return jnp.where(mask, diff, -jnp.inf)

def ssd_chunked_scan(xh, dt, a, bm, cm):
    bsz, seq = xh.shape[:2]
    nc = seq // SSD_CHUNK
    xd = (xh * dt[..., None]).reshape(bsz, nc, SSD_CHUNK, SSD_GROUPS, SSD_HPG, SSD_HEADDIM)
    ad = (dt * a).reshape(bsz, nc, SSD_CHUNK, SSD_GROUPS, SSD_HPG).transpose(0, 3, 4, 1, 2)
    bc = bm.reshape(bsz, nc, SSD_CHUNK, SSD_GROUPS, SSD_STATE)
    cc = cm.reshape(bsz, nc, SSD_CHUNK, SSD_GROUPS, SSD_STATE)
    a_cs = jnp.cumsum(ad, axis=-1)
    decay_in = jnp.exp(segsum(ad))
    cb = jnp.einsum('bclgn,bcsgn->bgcls', cc, bc)
    y_diag = jnp.einsum('bgcls,bgrcls,bcsgrp->bclgrp', cb, decay_in, xd)
    decay_to_end = jnp.exp(a_cs[..., -1:] - a_cs)
    chunk_states = jnp.einsum('bclgn,bgrcl,bclgrp->bcgrpn', bc, decay_to_end, xd)
    chunk_states = jnp.concatenate([jnp.zeros_like(chunk_states[:, :1]), chunk_states], axis=1)
    chunk_a = jnp.pad(a_cs[..., -1], ((0, 0), (0, 0), (0, 0), (1, 0)))
    decay_chunk = jnp.exp(segsum(chunk_a))
    carried = jnp.einsum('bgrzc,bcgrpn->bzgrpn', decay_chunk, chunk_states)[:, :-1]
    y_off = jnp.einsum('bclgn,bcgrpn,bgrcl->bclgrp', cc, carried, jnp.exp(a_cs))
    return (y_diag + y_off).reshape(bsz, seq, SSD_GROUPS, SSD_HPG, SSD_HEADDIM)

def _flip_seq(t):
    return jnp.flip(t, axis=1)

def ssd_mixer(u, w_in, conv_w, conv_b, dt_bias, a_log, d_skip, norm_w, w_out):
    bsz, seq, _ = u.shape
    proj = u @ w_in
    z = proj[..., :SSD_D_INNER]
    xbc = jax.nn.silu(dwconv_centred(proj[..., SSD_D_INNER:SSD_D_INNER + SSD_CONV_DIM], conv_w, conv_b))
    dt_raw = proj[..., SSD_D_INNER + SSD_CONV_DIM:].astype(jnp.float32)
    xh = xbc[..., :SSD_D_INNER].reshape(bsz, seq, SSD_GROUPS, SSD_HPG, SSD_HEADDIM)
    bm = xbc[..., SSD_D_INNER:SSD_D_INNER + SSD_BC_DIM].reshape(bsz, seq, SSD_GROUPS, SSD_STATE)
    cm = xbc[..., SSD_D_INNER + SSD_BC_DIM:].reshape(bsz, seq, SSD_GROUPS, SSD_STATE)
    dt = jax.nn.softplus(dt_raw + dt_bias.reshape(-1).astype(jnp.float32))
    dt = dt.reshape(bsz, seq, 2, SSD_GROUPS, SSD_HPG)
    a = -jnp.exp(a_log.astype(jnp.float32)).reshape(2, SSD_GROUPS, SSD_HPG)
    y_fwd = ssd_chunked_scan(xh, dt[:, :, 0], a[0], bm, cm)
    y_bwd = _flip_seq(ssd_chunked_scan(_flip_seq(xh), _flip_seq(dt[:, :, 1]), a[1], _flip_seq(bm), _flip_seq(cm)))
    y = y_fwd + y_bwd + xh * d_skip.reshape(SSD_GROUPS, SSD_HPG)[:, :, None]
    y = y.reshape(bsz, seq, SSD_D_INNER) * jax.nn.silu(z.astype(jnp.float32))
    yg = y.reshape(bsz, seq, SSD_GROUPS, SSD_D_INNER // SSD_GROUPS)
    yg = yg * lax.rsqrt(jnp.mean(yg * yg, axis=-1, keepdims=True) + NORM_EPS)
    y = yg.reshape(bsz, seq, SSD_D_INNER) * norm_w.astype(jnp.float32)
    return (y @ w_out).astype(u.dtype)

def _complex_linear_combine(e1, e2):
    a1r, a1i, b1r, b1i = e1
    a2r, a2i, b2r, b2i = e2
    return (a2r * a1r - a2i * a1i,
            a2r * a1i + a2i * a1r,
            a2r * b1r - a2i * b1i + b2r,
            a2r * b1i + a2i * b1r + b2i)

def s5_mixer(u, a_re, a_im, log_step, b_re, b_im, c_re, c_im, d_skip, w_glu, b_glu):
    bsz, seq, _ = u.shape
    uf = u.astype(jnp.float32)
    ug = uf.reshape(bsz, seq, S5_GROUPS, S5_GROUP)
    bu_re = jnp.einsum('blgh,gph->blgp', ug, b_re.astype(jnp.float32))
    bu_im = jnp.einsum('blgh,gph->blgp', ug, b_im.astype(jnp.float32))
    y_ssm = jnp.zeros((bsz, seq, S5_GROUPS, S5_GROUP), jnp.float32)
    for d in range(2):
        lr = a_re[d].astype(jnp.float32)
        li = a_im[d].astype(jnp.float32)
        step = jnp.exp(log_step[d].astype(jnp.float32))[:, None]
        mag = jnp.exp(lr * step)
        ang = li * step
        lb_re = mag * jnp.cos(ang)
        lb_im = mag * jnp.sin(ang)
        nr = lb_re - 1.0
        den = lr * lr + li * li
        q_re = (nr * lr + lb_im * li) / den
        q_im = (lb_im * lr - nr * li) / den
        drive_re = q_re * bu_re - q_im * bu_im
        drive_im = q_re * bu_im + q_im * bu_re
        dec_re = jnp.broadcast_to(lb_re, (1, seq, S5_GROUPS, S5_STATE))
        dec_im = jnp.broadcast_to(lb_im, (1, seq, S5_GROUPS, S5_STATE))
        _, _, st_re, st_im = lax.associative_scan(
            _complex_linear_combine, (dec_re, dec_im, drive_re, drive_im), axis=1, reverse=(d == 1))
        y_ssm = (y_ssm
                 + jnp.einsum('blgp,ghp->blgh', st_re, c_re[d].astype(jnp.float32))
                 - jnp.einsum('blgp,ghp->blgh', st_im, c_im[d].astype(jnp.float32)))
    y = y_ssm.reshape(bsz, seq, D_MODEL) + d_skip.astype(jnp.float32) * uf
    g = jax.nn.gelu(y)
    h = g @ w_glu + b_glu
    out = h[..., :D_MODEL] * jax.nn.sigmoid(h[..., D_MODEL:])
    return out.astype(u.dtype)

def conv_ffn(u, w_up, conv_w, conv_b, w_down):
    h = dwconv_centred(u @ w_up, conv_w, conv_b)
    gate = h[..., :FFN_HIDDEN]
    val = h[..., FFN_HIDDEN:]
    return ((jax.nn.silu(gate) * val) @ w_down).astype(u.dtype)

def per_layer_embed(h, p_i, norm_w, w_gate, w_proj):
    gate = jax.nn.sigmoid(rmsnorm(h, norm_w) @ w_gate)
    return ((p_i @ w_proj) * gate).astype(h.dtype)

def setup_inputs(seed: int = 0) -> dict:
    key = jax.random.key(seed)
    ks = iter(jax.random.split(key, 40))
    f32 = jnp.float32

    def nrm(shape, scale):
        return jax.random.normal(next(ks), shape, f32) * scale

    def gain(shape):
        return 1.0 + 0.02 * jax.random.normal(next(ks), shape, f32)

    x = nrm((BATCH, SEQ, D_MODEL), 1.0)
    p = nrm((DEPTH, BATCH, SEQ, PLE_DIM), 1.0)

    na, nb = N_LAYERS_A, N_LAYERS_B
    ssd_w_in = nrm((na, D_MODEL, SSD_IN_DIM), D_MODEL ** -0.5)
    ssd_conv_w = nrm((na, SSD_CONV, SSD_CONV_DIM), SSD_CONV ** -0.5)
    ssd_conv_b = nrm((na, SSD_CONV_DIM), 0.02)
    dt0 = jnp.exp(jax.random.uniform(next(ks), (na, 2, SSD_HEADS), f32,
                                     math.log(SSD_DT_MIN), math.log(SSD_DT_MAX)))
    ssd_dt_bias = dt0 + jnp.log(-jnp.expm1(-dt0))
    ssd_a_log = jnp.log(jax.random.uniform(next(ks), (na, 2, SSD_HEADS), f32, 1.0, 16.0))
    ssd_d = 1.0 + 0.1 * jax.random.normal(next(ks), (na, SSD_HEADS), f32)
    ssd_norm_w = gain((na, SSD_D_INNER))
    ssd_w_out = nrm((na, SSD_D_INNER, D_MODEL), SSD_D_INNER ** -0.5)

    s5_a_re = -0.5 + nrm((nb, 2, S5_GROUPS, S5_STATE), 0.01)
    s5_a_im = jnp.pi * jnp.arange(S5_STATE, dtype=f32) + nrm((nb, 2, S5_GROUPS, S5_STATE), 0.01)
    s5_log_step = jax.random.uniform(next(ks), (nb, 2, S5_GROUPS), f32,
                                     math.log(S5_STEP_MIN), math.log(S5_STEP_MAX))
    s5_b_re = nrm((nb, S5_GROUPS, S5_STATE, S5_GROUP), (2 * S5_GROUP) ** -0.5)
    s5_b_im = nrm((nb, S5_GROUPS, S5_STATE, S5_GROUP), (2 * S5_GROUP) ** -0.5)
    s5_c_re = nrm((nb, 2, S5_GROUPS, S5_GROUP, S5_STATE), 0.25)
    s5_c_im = nrm((nb, 2, S5_GROUPS, S5_GROUP, S5_STATE), 0.25)
    s5_d = 1.0 + 0.1 * jax.random.normal(next(ks), (nb, D_MODEL), f32)
    s5_w_glu = nrm((nb, D_MODEL, 2 * D_MODEL), D_MODEL ** -0.5)
    s5_b_glu = nrm((nb, 2 * D_MODEL), 0.02)

    mix_norm_w = gain((DEPTH, D_MODEL))
    ffn_norm_w = gain((DEPTH, D_MODEL))
    ffn_w_up = nrm((DEPTH, D_MODEL, 2 * FFN_HIDDEN), D_MODEL ** -0.5)
    ffn_conv_w = nrm((DEPTH, FFN_CONV, 2 * FFN_HIDDEN), FFN_CONV ** -0.5)
    ffn_conv_b = nrm((DEPTH, 2 * FFN_HIDDEN), 0.02)
    ffn_w_down = nrm((DEPTH, FFN_HIDDEN, D_MODEL), FFN_HIDDEN ** -0.5)

    ple_norm_w = gain((DEPTH, D_MODEL))
    ple_w_gate = nrm((DEPTH, D_MODEL, D_MODEL), D_MODEL ** -0.5)
    ple_w_proj = nrm((DEPTH, PLE_DIM, D_MODEL), PLE_DIM ** -0.5)
    final_norm_w = gain((D_MODEL,))

    return {
        'x': x, 'p': p,
        'ssd_w_in': ssd_w_in, 'ssd_conv_w': ssd_conv_w, 'ssd_conv_b': ssd_conv_b,
        'ssd_dt_bias': ssd_dt_bias, 'ssd_a_log': ssd_a_log, 'ssd_d': ssd_d,
        'ssd_norm_w': ssd_norm_w, 'ssd_w_out': ssd_w_out,
        's5_a_re': s5_a_re, 's5_a_im': s5_a_im, 's5_log_step': s5_log_step,
        's5_b_re': s5_b_re, 's5_b_im': s5_b_im, 's5_c_re': s5_c_re, 's5_c_im': s5_c_im,
        's5_d': s5_d, 's5_w_glu': s5_w_glu, 's5_b_glu': s5_b_glu,
        'mix_norm_w': mix_norm_w, 'ffn_norm_w': ffn_norm_w, 'ffn_w_up': ffn_w_up,
        'ffn_conv_w': ffn_conv_w, 'ffn_conv_b': ffn_conv_b, 'ffn_w_down': ffn_w_down,
        'ple_norm_w': ple_norm_w, 'ple_w_gate': ple_w_gate, 'ple_w_proj': ple_w_proj,
        'final_norm_w': final_norm_w,
    }

def reference(x, p,
              ssd_w_in, ssd_conv_w, ssd_conv_b, ssd_dt_bias, ssd_a_log, ssd_d, ssd_norm_w, ssd_w_out,
              s5_a_re, s5_a_im, s5_log_step, s5_b_re, s5_b_im, s5_c_re, s5_c_im, s5_d, s5_w_glu, s5_b_glu,
              mix_norm_w, ffn_norm_w, ffn_w_up, ffn_conv_w, ffn_conv_b, ffn_w_down,
              ple_norm_w, ple_w_gate, ple_w_proj,
              final_norm_w):
    h = x
    for i in range(DEPTH):
        u = rmsnorm(h, mix_norm_w[i])
        j = i // N_MIXERS
        if i % N_MIXERS == 0:
            mix = ssd_mixer(u, ssd_w_in[j], ssd_conv_w[j], ssd_conv_b[j], ssd_dt_bias[j],
                            ssd_a_log[j], ssd_d[j], ssd_norm_w[j], ssd_w_out[j])
        else:
            mix = s5_mixer(u, s5_a_re[j], s5_a_im[j], s5_log_step[j], s5_b_re[j], s5_b_im[j],
                           s5_c_re[j], s5_c_im[j], s5_d[j], s5_w_glu[j], s5_b_glu[j])
        h = h + mix
        h = h + conv_ffn(rmsnorm(h, ffn_norm_w[i]), ffn_w_up[i], ffn_conv_w[i], ffn_conv_b[i], ffn_w_down[i])
        h = h + per_layer_embed(h, p[i], ple_norm_w[i], ple_w_gate[i], ple_w_proj[i])
    return rmsnorm(h, final_norm_w)


_drawn_inputs = setup_inputs


def setup_inputs(seed=0):
    import zlib

    import numpy as np

    out = dict(_drawn_inputs(seed))
    spreads = {}
    factors = {'ssd_norm_w': 3.797,
     's5_a_re': 200.0,
     's5_b_glu': 45.819,
     'ffn_norm_w': 3.744,
     'ffn_conv_b': 3.902,
     'ple_norm_w': 200.0,
     'final_norm_w': 25.136,
     's5_a_im': 64.0,
     's5_log_step': 64.0,
     's5_b_re': 64.0,
     's5_b_im': 64.0,
     's5_c_re': 64.0,
     's5_c_im': 64.0,
     's5_d': 8.0}
    for name, (base, spread) in spreads.items():
        noise = np.random.default_rng([zlib.crc32(name.encode()), seed]).standard_normal(out[name].shape)
        drawn = base * np.exp(spread * noise) if base else spread * noise
        out[name] = jnp.asarray(drawn.astype(out[name].dtype))
    for name, factor in factors.items():
        out[name] = (out[name] * factor).astype(out[name].dtype)
    return out
```

```python
import concourse.bass as bass
from concourse import mybir
from contextlib import ExitStack

F32 = mybir.dt.float32
F32R = mybir.dt.float32r
ACT = mybir.ActivationFunctionType
ALU = mybir.AluOpType

P = 128
EPS = 1e-6
PI = 3.14159265358979
PI_BELOW = 3.1415925
TWO_PI_HI = 6.28125
TWO_PI_MID = 0.0019350051879882812
TWO_PI_LO = 2.0 * 3.141592653589793 - TWO_PI_HI - TWO_PI_MID
ROUND_MAGIC = 12582912.0


class Plan:

    def __init__(self, groups, ffn_pairs):
        self.tile, self.fill, self.unit = {}, {}, {}
        tiles = fills = 0

        def tile(name, n, streamed=False):
            nonlocal tiles, fills
            self.tile[name] = tiles
            tiles += n
            if not streamed:
                self.fill[name] = fills
                fills += n

        tile("params", 2)
        tile("x", 8)
        tile("dt", 1, True)
        tile("seq", 1)
        tile("sums", 1)
        tile("totals", 1)
        for g in range(groups):
            tile(("xbc", g), 6, True)
            tile(("z", g), 4, True)
            tile(("xseq", g), 4)
            tile(("bseq", g), 1)
            tile(("cb", g), 1)
            tile(("state", g), 6)
            tile(("yoff", g), 6)
            tile(("out", g), 8, True)
        for layer in range(2):
            if layer == 1:
                tile("c5", 8)
                tile("s5", 64)
                tile("glu", 16, True)
            tile(("up", layer), 4 * ffn_pairs, True)
            tile(("p", layer), 2)
            tile(("down", layer), 8, True)
            tile(("proj", layer), 8, True)
            tile(("gate", layer), 8, True)
        tile("final", 8)

        units = 0
        for name, n in ([("dt", 1)] + [(("ssd", g), 14) for g in range(groups)]
                        + [(("up", 0), 4 * ffn_pairs), (("down", 0), 24), (("proj", 0), 2), (("gate", 0), 8)]
                        + [("glu", 16), (("up", 1), 4 * ffn_pairs), (("down", 1), 24), (("proj", 1), 2),
                           (("gate", 1), 8)]):
            self.unit[name] = units
            units += n
        self.units = units


def bidir_hybrid_kernel(nc, A, out):
    _, SEQ, D = A["x"].shape
    KD = D // P
    SB = SEQ // P
    INNER = A["ssd_norm_w"].shape[1]
    HEADS = A["ssd_d"].shape[1]
    HD = INNER // HEADS
    GROUPS = 4
    HPG = HEADS // GROUPS
    GC = INNER // GROUPS
    GT = GC // P
    CONV_T = A["ssd_conv_b"].shape[1] // P
    XBC0 = INNER
    HID = A["ffn_w_down"].shape[1]
    HT = HID // P
    PAIRS = HT // 2
    PLE = A["p"].shape[3]
    PK = PLE // P
    TAU = 4
    NCH = SEQ // TAU
    S5G = A["s5_b_re"].shape[1]
    S5P = A["s5_b_re"].shape[2]
    S5H = A["s5_b_re"].shape[3]
    J = S5G * S5P // P
    NB = D // P
    BP = J // NB
    CH = 2 * S5H

    plan = Plan(GROUPS, PAIRS)
    T, FILL, U, UNITS = plan.tile, plan.fill, plan.unit, plan.units

    C_MIX, C_FFN, C_PLE, C_FIN = 0, 16, 32, 48
    C_BGLU, C_S5D, C_SSDN, C_CONVB = 56, 72, 80, 96
    C_CONVW = P
    C_FCW = 2 * P
    C_FCB = C_FCW + 2 * 3 * 2 * HT
    C_A = 5 * P
    C_STEP = 6 * P

    with ExitStack() as ctx:
        def sb(name, shape, dt=F32, where=ctx):
            return where.enter_context(nc.sbuf_tensor(name, shape, dt))

        def sem(name):
            return ctx.enter_context(nc.semaphore(name))

        h = sb("h", [P, KD, SEQ])
        w_raw = sb("w_raw", [P, 2, 1024])
        w_hi = [sb(f"w_hi{i}", [P, 1024], F32R) for i in range(2)]
        w_lo = [sb(f"w_lo{i}", [P, 1024], F32R) for i in range(2)]
        par = sb("par", [P, 7 * P])
        ones = sb("ones", [P, P])
        eye = sb("eye", [P, P])
        le = sb("le", [P, P])
        ge = sb("ge", [P, P])
        lt = sb("lt", [P, P])
        gt = sb("gt", [P, P])
        rstd = sb("rstd", [P, SEQ])
        var = sb("var", [P, SEQ])
        sq = sb("sq", [P, 2, SEQ])
        cin = sb("cin", [P, 2, SEQ + 4])
        cc = sb("cc", [P, 4, SEQ])
        d_row = sb("d_row", [P, HEADS])
        d_col = sb("d_col", [P, HEADS // 2])
        hvec = sb("hvec", [2 * HEADS, 4])

        layer0 = ExitStack()
        uh0 = sb("uh0", [P, KD, SEQ], F32R, layer0)
        ul0 = sb("ul0", [P, KD, SEQ], F32R, layer0)
        start = ExitStack()
        x_in = sb("x_in", [P, SB, D], where=start)
        stage = sb("stage", [P, 7, P], where=start)
        step_in = sb("step_in", [2 * J, 2], where=start)
        start.close()
        ssd = ExitStack()
        xT = sb("xT", [P, GT, SEQ], where=ssd)
        bT = sb("bT", [P, SEQ], where=ssd)
        cT = sb("cT", [P, SEQ], where=ssd)
        xseq = sb("xseq", [P, SB, GC], where=ssd)
        bseq = sb("bseq", [P, SB, P], where=ssd)
        cbT = sb("cbT", [P, SEQ], where=ssd)
        zs = sb("zs", [P, GT, SEQ], where=ssd)
        xd = sb("xd", [P, 2, GC], where=ssd)
        car = sb("car", [P, 2, SB - 1, GC], where=ssd)
        yo = sb("yo", [P, SB, GC], where=ssd)
        ytmp = sb("ytmp", [P, GC], where=ssd)
        rr = sb("rr", [P, 2, 2, SB, P], where=ssd)
        wf = sb("wf", [P, 2, SB, P], where=ssd)
        wb = sb("wb", [P, 2, SB, P], where=ssd)
        mm = sb("mm", [P, 2, 2, SEQ], where=ssd)
        dt_seq = sb("dt_seq", [P, SB, 2 * HEADS], where=ssd)
        ad_seq = sb("ad_seq", [P, SB, 2 * HEADS], where=ssd)
        epq = sb("epq", [P, 2, SB, 2 * HEADS], where=ssd)
        etot = sb("etot", [P, SB, 2 * HEADS], where=ssd)
        yh = sb("yh", [P, GT, SEQ], F32R, ssd)
        yl = sb("yl", [P, GT, SEQ], F32R, ssd)
        dtT = mm[0:2 * HEADS, 0, 0, :]
        adT = mm[0:2 * HEADS, 0, 1, :]
        spz = mm[0:2 * HEADS, 1, 0, :]
        spw = mm[0:2 * HEADS, 1, 1, :]
        speq = wf[0:2 * HEADS, 0].rearrange("p c l -> p (c l)")
        ssd.close()

        def ffn_memory(layer, where):
            m = ExitStack()
            gh = sb(f"gh{layer}", [P, HT, SEQ], F32R, m)
            gl = sb(f"gl{layer}", [P, HT, SEQ], F32R, m)
            keep = sb(f"p_in{layer}", [P, SB, PLE], where=m)
            ph = sb(f"ph{layer}", [P, PK, SEQ], F32R, m)
            pl = sb(f"pl{layer}", [P, PK, SEQ], F32R, m)
            m.close()
            m = ExitStack()
            pp = sb(f"pproj{layer}", [P, KD, SEQ], where=m)
            m.close()
            return gh, gl, keep, ph, pl, pp

        ffn0 = ffn_memory(0, layer0)
        layer0.close()

        s5 = ExitStack()
        u5 = sb("u5", [P, KD, SEQ], where=s5)
        c_in = sb("c_in", [P, 4, NB, P], where=s5)
        s5.close()
        s5 = ExitStack()
        sb("u5_again", [P, KD, SEQ], where=s5)
        cw = sb("cw", [P, 2, 2, J, S5H], where=s5)
        b5 = sb("b5", [P, 2, J, S5H], where=s5)
        pw = sb("pw", [P, TAU + 1, 2, 4, BP, S5H], where=s5)
        px = sb("px", [P, 2, 4 * BP, S5H], where=s5)
        py = sb("py", [P, 2, 4 * BP, S5H], where=s5)
        cblk = sb("cblk", [P, 2, 2, BP, TAU + 1, CH], where=s5)
        vblk = sb("vblk", [P, 2, 2, BP, TAU, CH], where=s5)
        vT = sb("vT", [P, 2, 2, BP, P], where=s5)
        kT = sb("kT", [P, BP, P], where=s5)
        ulift = sb("ulift", [P, BP, NCH], where=s5)
        rot = sb("rot", [P, 2, 2 * BP, NCH], where=s5)
        m4 = sb("m4", [P, 2 * BP, NCH], where=s5)
        zz = sb("zz", [P, 2, 2 * BP, NCH], where=s5)
        ta = sb("ta", [P, 2 * BP, NCH], where=s5)
        tb = sb("tb", [P, 2 * BP, NCH], where=s5)
        xs = sb("xs", [P, 2, 2, BP, NCH + 1], where=s5)
        y5 = sb("y5", [P, SEQ], where=s5)
        smask = sb("smask", [P, 2, NCH], where=s5)
        v5 = sb("v5", [P, 16, 2 * J], where=s5)
        lamx = sb("lamx", [P, 2, NB, 4 * BP], where=s5)
        m4v = sb("m4v", [P, 2 * J], where=s5)
        cst = zz[:].rearrange("p a x k -> p (a x k)").rearrange(
            "p (c b j q) -> p c b j q", c=4, b=NB, j=BP)
        tn = sb("tn", [P, 2, 7, 2 * J], where=s5)
        s5.close()
        layer1 = ExitStack()
        uh1 = sb("uh1", [P, KD, SEQ], F32R, layer1)
        ul1 = sb("ul1", [P, KD, SEQ], F32R, layer1)
        glu = ExitStack()
        gh5 = sb("gh5", [P, KD, SEQ], F32R, glu)
        gl5 = sb("gl5", [P, KD, SEQ], F32R, glu)
        glu.close()
        ffn1 = ffn_memory(1, layer1)
        layer1.close()
        last = ExitStack()
        hn = sb("hn", [P, KD, SEQ], where=last)
        o_sb = sb("o_sb", [P, SB, D], where=last)
        last.close()
        UH, UL = [uh0, uh1], [ul0, ul1]
        FFN = [ffn0, ffn1]

        ring = ctx.enter_context(nc.psum_tensor("ring", [P, 4, SEQ], F32))
        pe_e = ctx.enter_context(nc.psum_tensor("pe_e", [P, 2, SEQ], F32))
        pe_y = ctx.enter_context(nc.psum_tensor("pe_y", [P, SEQ], F32))
        pe_s = ctx.enter_context(nc.psum_tensor("pe_s", [P, SEQ], F32))

        loaded = [sem("w_loaded0"), sem("w_loaded1")]
        hi_done, lo_done = sem("w_hi_done"), sem("w_lo_done")
        unit_done = sem("unit_done")
        filled, evac = sem("tile_filled"), sem("tile_evacuated")
        in_x, in_par, in_small = sem("x_loaded"), sem("params_loaded"), sem("small_loaded")
        masks = sem("masks_ready")
        stage_zero = sem("stage_zeroed")
        c5_half, cw_done = sem("c_upper_taken"), sem("cq_done")
        zz_r, p_lo = sem("turned_last"), sem("p_lo")
        step_x = sem("step_spread")
        sq_done, sq_used = sem("square_done"), sem("square_summed")
        var_done, std_done, rstd_done = sem("variance_done"), sem("std_done"), sem("rstd_done")
        h_upd = sem("h_updated")
        uh_done, ul_done = sem("u_hi_done"), sem("u_lo_done")
        dt_done = sem("dt_done")
        sp_step = sem("softplus_step")
        dtx, adt = sem("dt_softplus"), sem("dt_a_done")
        e_done = sem("decays_exp_done")
        eq_done = sem("decay_dt_done")
        tap0, taps, silu = sem("conv_tap0"), sem("conv_taps"), sem("conv_silu")
        z_silu = sem("z_silu")
        xd_done, car_mul = sem("x_decayed"), sem("carry_decayed")
        yo_add = sem("yoff_added")
        r_done, e_full, exp_done = sem("masked_logs"), sem("exponents_filled"), sem("decay_exp")
        w_done, m_done, m_half = sem("dt_weights"), sem("m_done"), sem("m_half")
        y_full, y_skip, gated = sem("y_filled"), sem("y_skip_added"), sem("y_gated")
        gsq, gsq_used = sem("group_square"), sem("group_summed")
        gvar, gstd, grstd = sem("group_variance"), sem("group_std"), sem("group_rstd")
        yn_done, yh_done, yl_done = sem("y_normed"), sem("y_hi"), sem("y_lo")
        f_c0, f_taps, f_silu = sem("ffn_tap0"), sem("ffn_taps"), sem("ffn_silu")
        f_gv, f_gh, f_gl = sem("ffn_product"), sem("ffn_product_hi"), sem("ffn_product_lo")
        p_loaded = [sem("p0_loaded"), sem("p1_loaded")]
        p_hi = sem("p_hi")
        g_sig, g_mul = sem("gate_sigmoid"), sem("gate_product")
        u5_done = sem("s5_input")
        v_act, v_dve = sem("s5_vec_act"), sem("s5_vec_dve")
        c_loaded, b_loaded = sem("c_loaded"), sem("b_loaded")
        s5_zero = sem("s5_zeroed")
        pw0 = sem("power0_ready")
        pw_x, pw_r = sem("power_products"), sem("power_ready")
        blk = sem("block_diagonals")
        rot_x, rot_r = sem("rotation_products"), sem("rotation_ready")
        lift = sem("u_lifted")
        k_full, k_evac = sem("kernel_filled"), sem("kernel_evacuated")
        spin = sem("rotated")
        scan = sem("scanned")
        xs_r = sem("states_ready")
        y5_full, y5_un, y5_skip, y5_gelu = (sem("s5_y_filled"), sem("s5_y_unlifted"), sem("s5_y_skip"),
                                            sem("s5_gelu"))
        m4_r = sem("decay_row_ready")
        g5_hi, g5_lo = sem("g_hi"), sem("g_lo")
        glu_sig, glu_mul = sem("glu_sigmoid"), sem("glu_product")
        hn_done = sem("h_normed")
        stored = sem("output_stored")

        def bank(t):
            return ring[:, t % 4, :]

        def col(c):
            return par[:, c:c + 1]

        def dcol(c):
            return par[:, bass.ds(c, 1)]

        def h_ready(r, m):
            if r == 0:
                return evac, T["x"] + m + 1
            if r == 1:
                return evac, T[("out", GROUPS - 1)] + m + 1
            if r in (2, 5):
                return evac, T[("down", r // 3)] + m + 1
            return h_upd, {3: 0, 4: KD, 6: 2 * KD}[r] + m + 1

        SPLIT = {0: 0, 1: 1, 2: 2, 4: 3, 5: 4}
        NORM_COL = {0: C_MIX, 1: C_FFN, 2: C_PLE, 3: C_MIX + KD, 4: C_FFN + KD, 5: C_PLE + KD, 6: C_FIN}

        def unit_size(u):
            for name in ("dt",):
                if u == U[name]:
                    return KD * 2 * HEADS
            for layer in range(2):
                k = u - U[("down", layer)]
                if 0 <= k < 24 and k % 6 == 5:
                    return 512
            return 1024

        def loads_by(u):
            two = [U[("ssd", g)] + 4 + kg for g in range(GROUPS) for kg in range(2)]
            return 16 * (u // 2 + 1) + 16 * sum(1 for t in two if t <= u and t % 2 == u % 2)

        def part(buf, u, k):
            n = unit_size(u)
            b = buf[:, u % 2, 0:n] if buf is w_raw else buf[u % 2][:, 0:n]
            return b.rearrange("p (k n) -> p k n", k=k)

        block = ctx.enter_context(nc.Block())

        @block.sync
        def _(sp):
            def load(u, src, at=0, k=4):
                if u >= 2:
                    sp.wait_ge(lo_done, at + (u - 1))
                sp.dma_start(part(w_raw, u, k), src).then_inc(loaded[u % 2], 16)

            def rows(w, k0, nk, c0, nc_):
                return w[k0 * P:(k0 + nk) * P, c0:c0 + nc_].rearrange("(k p) n -> p k n", p=P)

            sp.dma_start(x_in[:], A["x"][0].rearrange("(b p) d -> p b d", p=P)).then_inc(in_x, 16)

            sp.wait_ge(stage_zero, 1)

            def vec(group, r0, ap):
                sp.dma_start(stage[r0:r0 + ap.shape[0], group, :], ap).then_inc(in_par, 16)

            vec(0, C_MIX, A["mix_norm_w"].rearrange("l (c p) -> (l c) p", p=P))
            vec(0, C_FFN, A["ffn_norm_w"].rearrange("l (c p) -> (l c) p", p=P))
            vec(0, C_PLE, A["ple_norm_w"].rearrange("l (c p) -> (l c) p", p=P))
            vec(0, C_FIN, A["final_norm_w"].rearrange("(c p) -> c p", p=P))
            vec(0, C_BGLU, A["s5_b_glu"].rearrange("l (c p) -> (l c) p", p=P))
            vec(0, C_S5D, A["s5_d"].rearrange("l (c p) -> (l c) p", p=P))
            vec(0, C_SSDN, A["ssd_norm_w"].rearrange("l (c p) -> (l c) p", p=P))
            vec(0, C_CONVB, A["ssd_conv_b"].rearrange("l (c p) -> (l c) p", p=P))
            vec(1, 0, A["ssd_conv_w"].rearrange("l t (c p) -> (l t c) p", p=P))
            fcw = A["ffn_conv_w"].rearrange("l t (c p) -> (l t c) p", p=P)
            vec(2, 0, fcw[0:P])
            vec(3, 0, fcw[P:2 * P])
            vec(4, 0, fcw[2 * P:])
            vec(4, C_FCB - 4 * P, A["ffn_conv_b"].rearrange("l (c p) -> (l c) p", p=P))
            vec(5, 0, A["s5_a_re"].rearrange("l d (j g) p -> (l d j) (g p)", g=2))
            vec(5, 2 * J, A["s5_a_im"].rearrange("l d (j g) p -> (l d j) (g p)", g=2))
            sp.dma_start(step_in[:], A["s5_log_step"].rearrange("l d (j g) -> (l d j) g", g=2)).then_inc(in_par, 16)
            sp.dma_start(hvec[:, 0:1], A["ssd_dt_bias"].rearrange("l d (h a) -> (l d h) a", a=1)).then_inc(in_small, 16)
            sp.dma_start(hvec[:, 1:2], A["ssd_a_log"].rearrange("l d (h a) -> (l d h) a", a=1)).then_inc(in_small, 16)
            sp.dma_start(d_row[:], A["ssd_d"][0].partition_broadcast(P)).then_inc(in_small, 16)
            load(U["dt"], rows(A["ssd_w_in"][0], 0, KD, XBC0 + CONV_T * P, 2 * HEADS), k=KD)

            w_in = A["ssd_w_in"][0]
            bc = w_in[:, XBC0 + INNER:XBC0 + INNER + 2 * GROUPS * P].rearrange(
                "(k p) (two n) -> p k two n", p=P, two=2)

            def ssd_loads(g):
                u = U[("ssd", g)]
                for i in range(2):
                    for kg in range(2):
                        load(u + 2 * i + kg, rows(w_in, 4 * kg, 4, XBC0 + g * GC + 256 * i, 256))
                for kg in range(2):
                    if u + 4 + kg >= 2:
                        sp.wait_ge(lo_done, u + 4 + kg - 1)
                    dst = w_raw[:, (u + 4 + kg) % 2, :].rearrange("p (k two n) -> p k two n", k=4, two=2)
                    for two in range(2):
                        sp.dma_start(dst[:, :, two, :], bc[:, 4 * kg:4 * kg + 4, two, g * P:(g + 1) * P]
                                     ).then_inc(loaded[(u + 4 + kg) % 2], 16)
                for i in range(2):
                    for kg in range(2):
                        load(u + 6 + 2 * i + kg, rows(w_in, 4 * kg, 4, g * GC + 256 * i, 256))
                for i in range(4):
                    load(u + 10 + i, rows(A["ssd_w_out"][0], GT * g, GT, 256 * i, 256))

            ssd_loads(0)
            for g in range(1, GROUPS):
                ssd_loads(g)

            for layer in range(2):
                if layer == 1:
                    u = U["glu"]
                    w = A["s5_w_glu"][0]
                    for kg in range(2):
                        load(u + kg, rows(w, 4 * kg, 4, 0, 256))
                    sp.wait_ge(h_upd, KD)
                    for a, name in enumerate(("s5_c_re", "s5_c_im")):
                        for d in range(2):
                            for half in range(2):
                                sp.dma_start(c_in[:, 2 * a + d, :, 64 * half:64 * half + 64],
                                             A[name][0, d].rearrange("(b g) h p -> (g h) b p", b=NB)
                                             ).then_inc(c_loaded, 16)
                    sp.wait_ge(evac, T["c5"] + 8)
                    for a, name in enumerate(("s5_b_re", "s5_b_im")):
                        sp.dma_start(b5[:, a, :, :], A[name][0].rearrange("(j g) p h -> (g p) j h", g=2)
                                     ).then_inc(b_loaded, 16)
                    for i in range(4):
                        for half in range(2):
                            for kg in range(2):
                                if i or half:
                                    load(u + 4 * i + 2 * half + kg, rows(w, 4 * kg, 4, half * D + 256 * i, 256))
                u = U[("up", layer)]
                wk = A["ffn_w_up"][layer].rearrange("(k p) n -> p k n", p=P)
                with sp.Fori(0, PAIRS) as i:
                    for half in range(2):
                        for kg in range(2):
                            load(u + 2 * half + kg, wk[:, 4 * kg:4 * kg + 4, bass.ds(i * 256 + half * HID, 256)],
                                 at=i * 4)
                sp.wait_ge(ul_done, (2, 4)[layer] * KD)
                sp.dma_start(FFN[layer][2][:], A["p"][layer, 0].rearrange("(b q) n -> q b n", q=P)
                             ).then_inc(p_loaded[layer], 16)
                u = U[("down", layer)]
                for i in range(4):
                    for kg in range(6):
                        nk = min(4, HT - 4 * kg)
                        load(u + 6 * i + kg, rows(A["ffn_w_down"][layer], 4 * kg, nk, 256 * i, 256), k=nk)
                for i in range(2):
                    load(U[("proj", layer)] + i, rows(A["ple_w_proj"][layer], 0, PK, 512 * i, 512), k=PK)
                for i in range(4):
                    for kg in range(2):
                        load(U[("gate", layer)] + 2 * i + kg, rows(A["ple_w_gate"][layer], 4 * kg, 4, 256 * i, 256))

            o_v = out[0].rearrange("(b p) d -> p b d", p=P)
            for b in range(SB):
                sp.wait_ge(evac, T["final"] + 2 * b + 2)
                sp.dma_start(o_v[:, b, :], o_sb[:, b, :]).then_inc(stored, 16)
            sp.wait_ge(stored, 16 * SB)

        @block.gpsimd
        def _(pool):
            pool.memset(ones[:], 1.0).then_inc(masks, 1)
            for m in (le, ge, lt, gt):
                pool.memset(m[:], 1.0).then_inc(masks, 1)
            pool.memset(eye[:], 0.0).then_inc(masks, 1)
            pool.wait_ge(masks, 6)
            for m, sign, base in ((le, 1, 0), (ge, -1, 0), (lt, 1, -1), (gt, -1, -1)):
                pool.affine_select(out=m[:], in_=m[:], compare_op=ALU.is_ge, fill=0.0, base=base,
                                   pattern=[[sign, P]], channel_multiplier=-sign).then_inc(masks, 1)
            pool.affine_select(out=eye[:], in_=eye[:], compare_op=ALU.not_equal, fill=1.0, base=0,
                               pattern=[[-1, P]], channel_multiplier=1).then_inc(masks, 1)

            pool.wait_ge(evac, T["c5"] + 8)
            pool.memset(cblk[:], 0.0).then_inc(s5_zero, 1)
            pool.memset(vblk[:], 0.0).then_inc(s5_zero, 1)
            pool.memset(xs[:], 0.0).then_inc(s5_zero, 1)
            pool.memset(smask[:], 1.0).then_inc(s5_zero, 1)
            pool.wait_ge(s5_zero, 4)
            pool.memset(smask[:, 0, 0:1], 0.0).then_inc(s5_zero, 1)
            pool.memset(smask[:, 1, NCH - 1:NCH], 0.0).then_inc(s5_zero, 1)
            pool.wait_ge(u5_done, KD)
            pool.wait_ge(s5_zero, 6)
            with pool.Fori(0, NB) as b:
                pool.wait_ge(y5_full, b + 1)
                for j in range(BP):
                    for s in range(TAU):
                        if j or s:
                            pool.wait_ge(lift, b * 16 + (TAU * j + s))
                        pool.tensor_copy(ulift[CH * s:CH * s + CH, j, :],
                                         u5[CH * j:CH * j + CH, bass.ds(b, 1), s::TAU].rearrange(
                                             "p b k -> p (b k)")).then_inc(lift, 1)

        @block.scalar
        def _(act):
            def hi(u, at=0, mul=0):
                if u >= UNITS:
                    return
                act.wait_ge(loaded[u % 2], loads_by(u) + at * 8)
                if u >= 2:
                    act.wait_ge(unit_done, at + (u - 1))
                n = unit_size(u)
                act.activation(w_hi[u % 2][:, 0:n], w_raw[:, u % 2, 0:n], ACT.Copy).then_inc(hi_done, 1)

            rounded = [-1]

            def hi_to(u):
                while rounded[0] < u:
                    rounded[0] += 1
                    hi(rounded[0])

            def squares(r, m):
                act.wait_ge(*h_ready(r, m))
                if 8 * r + m >= 2:
                    act.wait_ge(sq_used, KD * r + m - 1)
                act.activation(sq[:, m % 2, :], h[:, m, :], ACT.Square).then_inc(sq_done, 1)

            def u_hi(r, m, uh):
                act.wait_ge(*h_ready(r, m))
                act.activation(uh[:, m, :], h[:, m, :], ACT.Identity, scale=col(NORM_COL[r] + m)).then_inc(uh_done, 1)

            def std(r):
                act.wait_ge(var_done, r + 1)
                act.activation(var[:], var[:], ACT.Sqrt).then_inc(std_done, 1)

            hi_to(0)
            act.wait_ge(evac, 2)
            for m in range(KD):
                squares(0, m)
                u_hi(0, m, uh0)
            std(0)
            hi_to(1)
            act.wait_ge(in_small, 48)
            act.activation(hvec[:, 2:3], hvec[:, 1:2], ACT.Exp).then_inc(dtx, 1)
            act.wait_ge(evac, T["dt"] + 1)
            act.activation(dtT, dtT, ACT.Identity, bias=hvec[:, 0:1]).then_inc(dtx, 1)
            act.wait_ge(dtx, 2)
            act.activation(spz, dtT, ACT.Abs).then_inc(dtx, 1)
            act.wait_ge(dtx, 3)
            act.activation(spz, spz, ACT.Exp, scale=-1.0).then_inc(dtx, 1)
            act.wait_ge(sp_step, 1)
            act.activation(adT, spw, ACT.Ln).then_inc(dtx, 1)
            act.wait_ge(evac, T["sums"] + 1)
            act.activation(epq[:], epq[:], ACT.Exp).then_inc(e_done, 1)
            act.wait_ge(evac, T["totals"] + 1)
            act.activation(etot[:], etot[:], ACT.Exp).then_inc(e_done, 1)

            for g in range(GROUPS):
                u = U[("ssd", g)]
                for i in range(3):
                    hi_to(u + 2 * i + 3)
                    chans = [g * GT + 2 * i, g * GT + 2 * i + 1] if i < 2 else [INNER // P + g, INNER // P + GROUPS + g]
                    for j in range(2):
                        q = 6 * g + 2 * i + j
                        act.wait_ge(evac, T[("xbc", g)] + 2 * i + j + 1)
                        if q >= 4:
                            act.wait_ge(silu, q - 3)
                        act.activation(cc[:, q % 4, :], cin[:, q % 2, 0:SEQ], ACT.Identity,
                                       scale=col(C_CONVW + chans[j]), bias=col(C_CONVB + chans[j])).then_inc(tap0, 1)
                    hi_to(u + 2 * i + 4)
                    if g >= 1 and i == 0:
                        act.wait_ge(yl_done, GT * g)
                    for j in range(2):
                        q = 6 * g + 2 * i + j
                        dst = xT[:, 2 * i + j, :] if i < 2 else (bT, cT)[j][:]
                        act.wait_ge(taps, 8 * (3 * g + i) + 6 + j + 1)
                        act.activation(dst, cc[:, q % 4, :], ACT.Silu).then_inc(silu, 1)
                for i in range(2):
                    hi_to(min(u + 6 + 2 * i + 4, u + 11))
                    for j in range(2):
                        act.wait_ge(evac, T[("z", g)] + 2 * i + j + 1)
                        act.activation(zs[:, 2 * i + j, :], zs[:, 2 * i + j, :], ACT.Silu).then_inc(z_silu, 1)
                for hp in range(HPG // 2 + 1):
                    if hp < HPG // 2:
                        n = GT * g + hp
                        act.wait_ge(e_full, n + 1)
                        if n >= 2:
                            act.wait_ge(y_full, n - 1)
                        act.activation(mm[:, n % 2, :, :], pe_e[:], ACT.Exp).then_inc(exp_done, 1)
                    if hp >= 1:
                        n = GT * g + hp - 1
                        act.wait_ge(gated, n + 1)
                        if n >= 2:
                            act.wait_ge(gsq_used, n - 1)
                        act.activation(sq[:, n % 2, :], xT[:, hp - 1, :], ACT.Square).then_inc(gsq, 1)
                act.wait_ge(gvar, g + 1)
                act.activation(var[:], var[:], ACT.Sqrt).then_inc(gstd, 1)
                for m in range(GT):
                    act.wait_ge(yn_done, GT * g + m + 1)
                    act.activation(yh[:, m, :], zs[:, m, :], ACT.Copy).then_inc(yh_done, 1)
                for i in range(4):
                    hi_to(u + 10 + i + 2)
                    if g == GROUPS - 1:
                        for m in (2 * i, 2 * i + 1):
                            squares(1, m)
                            u_hi(1, m, uh0)

            for layer in range(2):
                gh, gl, p_in, ph, pl, pproj = FFN[layer]
                if layer == 1:
                    act.wait_ge(rstd_done, 4)

                    def vec(dst, src, f, need, scale=1.0):
                        if need:
                            act.wait_ge(v_dve, need)
                        act.activation(v5[:, dst, :], src, f, scale=scale).then_inc(v_act, 1)

                    vec(0, par[:, C_STEP:C_STEP + 2 * J], ACT.Exp, 0)
                    vec(1, v5[:, 1, :], ACT.Exp, 1)
                    vec(2, v5[:, 5, :], ACT.Sin, 8)
                    vec(3, v5[:, 5, :], ACT.Sin, 8, 0.5)
                    act.sem_inc(blk, 1)
                    act.sem_inc(y5_gelu, 1)
                    with act.Fori(0, NB) as b:
                        act.wait_ge(b_loaded, 32)
                        act.wait_ge(cw_done, 1)
                        act.wait_ge(blk, b * 16 + 1)
                        for a in range(2):
                            for d in range(2):
                                act.activation(pw[:, 0, a, d, :, :], cw[:, a, d, bass.ds(b * BP, BP), :],
                                               ACT.Copy).then_inc(pw0, 1)
                                act.activation(pw[:, 0, a, 2 + d, :, :], b5[:, a, bass.ds(b * BP, BP), :],
                                               ACT.Copy).then_inc(pw0, 1)
                        act.wait_ge(pw_r, b * (2 * TAU) + 2 * TAU)
                        act.wait_ge(s5_zero, 6)
                        act.wait_ge(y5_full, b + 1)
                        for half in range(2):
                            rows = slice(64 * half, 64 * half + 64)
                            chs = slice(S5H * half, S5H * half + S5H)
                            for a in range(2):
                                for d in range(2):
                                    dst = cblk[rows, a, d, :, ::(1, -1)[d], chs]
                                    act.activation(dst.rearrange("p j t h -> p t j h"), pw[rows, :, a, d, :, :],
                                                   ACT.Copy, scale=(1.0, -1.0)[a]).then_inc(blk, 1)
                                    dst = vblk[rows, a, d, :, ::(-1, 1)[d], chs]
                                    act.activation(dst.rearrange("p j t h -> p t j h"), pw[rows, 0:TAU, a, 2 + d, :, :],
                                                   ACT.Copy).then_inc(blk, 1)
                        act.wait_ge(y5_full, b + 2)
                        act.wait_ge(y5_gelu, b + 1)
                        for j in range(BP):
                            for s in range(TAU):
                                act.activation(y5[CH * j:CH * j + CH, s::TAU], pe_y[CH * s:CH * s + CH,
                                               j * NCH:(j + 1) * NCH], ACT.Copy).then_inc(y5_un, 1)
                        act.wait_ge(y5_skip, b + 1)
                        act.activation(u5[:, bass.ds(b, 1), :].rearrange("p b t -> p (b t)"), y5[:],
                                       ACT.Gelu_apprx_tanh).then_inc(y5_gelu, 1)
                    act.wait_ge(y5_gelu, NB + 1)
                    for m in range(KD):
                        act.activation(gh5[:, m, :], u5[:, m, :], ACT.Copy).then_inc(g5_hi, 1)
                    u = U["glu"]
                    for i in range(4):
                        for half in range(2):
                            hi_to(u + 4 * i + 2 * half + 3)
                            if half:
                                for j in range(2):
                                    act.wait_ge(evac, T["glu"] + 4 * i + 2 + j + 1)
                                    act.activation(cc[:, 2 + j, :], cc[:, 2 + j, :], ACT.Sigmoid).then_inc(glu_sig, 1)
                        if i == 0:
                            act.wait_ge(g5_lo, KD)
                        for m in (2 * i, 2 * i + 1):
                            squares(4, m)
                            u_hi(4, m, uh1)
                std(1 + 3 * layer)
                u, t = U[("up", layer)], T[("up", layer)]
                hi_to(u + 2)
                done = layer * HT
                with act.Fori(0, PAIRS) as i:
                    for half in range(2):
                        hi(u + 2 * half + 3, at=i * 4)
                        for j in range(2):
                            act.wait_ge(evac, i * 4 + (t + 2 * half + j + 1))
                            act.wait_ge((f_gv, f_gl)[half], i * 2 + (done + j + 1))
                            c = 2 * 3 * HT * layer + half * HT + j
                            act.activation(cc[:, 2 * half + j, :], cin[:, j, 1:1 + SEQ], ACT.Identity,
                                           scale=dcol(i * 2 + (C_FCW + c)),
                                           bias=dcol(i * 2 + (C_FCB + 2 * HT * layer + half * HT + j))
                                           ).then_inc(f_c0, 1)
                        hi(u + 2 * half + 4, at=i * 4)
                        for j in range(2):
                            if half == 0:
                                act.wait_ge(f_taps, i * 8 + (4 * done + 2 + j + 2))
                                act.activation(cc[:, j, :], cc[:, j, :], ACT.Silu).then_inc(f_silu, 1)
                            else:
                                act.wait_ge(f_gv, i * 2 + (done + j + 3))
                                act.activation(gh[:, bass.ds(i * 2 + j, 1), :].rearrange("p a t -> p (a t)"),
                                               cc[:, 2 + j, :], ACT.Copy).then_inc(f_gh, 1)
                rounded[0] = U[("down", layer)] + 2
                for k in range(PK):
                    act.wait_ge(evac, T[("p", layer)] + k + 1)
                    act.activation(ph[:, k, :], cc[:, k, :], ACT.Copy).then_inc(p_hi, 1)
                u = U[("down", layer)]
                r = 2 + 3 * layer
                for i in range(4):
                    hi_to(u + 6 * i + 7)
                    for m in (2 * i, 2 * i + 1):
                        squares(r, m)
                        u_hi(r, m, UH[layer])
                std(r)
                for i in range(2):
                    hi_to(U[("proj", layer)] + i + 2)
                u = U[("gate", layer)]
                for i in range(4):
                    hi_to(u + 2 * i + 3)
                    for m in (2 * i, 2 * i + 1):
                        act.wait_ge(evac, T[("gate", layer)] + m + 1)
                        act.activation(cc[:, m % 4, :], cc[:, m % 4, :], ACT.Sigmoid).then_inc(g_sig, 1)
                    hi_to(min(u + 2 * i + 4, u + 9))
                    for m in (2 * i, 2 * i + 1):
                        squares(r + 1, m)
                std(r + 1)

        @block.vector
        def _(dve):
            def lo(u, at=0):
                if u >= UNITS:
                    return
                dve.wait_ge(hi_done, at + (u + 1))
                n = unit_size(u)
                dve.tensor_tensor(w_lo[u % 2][:, 0:n], w_raw[:, u % 2, 0:n], w_hi[u % 2][:, 0:n].bitcast(F32),
                                  ALU.subtract).then_inc(lo_done, 1)

            split = [-1]

            def lo_to(u):
                while split[0] < u:
                    split[0] += 1
                    lo(split[0])

            def u_lo(r, m, uh, ul):
                dve.wait_ge(uh_done, KD * SPLIT[r] + m + 1)
                dve.wait_ge(*h_ready(r, m))
                dve.scalar_tensor_tensor(out=ul[:, m, :], in0=h[:, m, :], scalar=col(NORM_COL[r] + m),
                                         in1=uh[:, m, :].bitcast(F32), op0=ALU.mult, op1=ALU.subtract
                                         ).then_inc(ul_done, 1)

            def rstd_of(r):
                dve.wait_ge(sq_used, KD * r + KD)
                dve.tensor_scalar(var[:], pe_s[:], 1.0 / D, EPS, ALU.mult, ALU.add).then_inc(var_done, 1)
                dve.wait_ge(std_done, r + 1)
                dve.reciprocal(rstd[:], var[:]).then_inc(rstd_done, 1)
                dve.wait_ge(rstd_done, r + 1)

            def take(name, k, dst):
                dve.wait_ge(filled, FILL[name] + k + 1)
                dve.tensor_copy(dst, bank(T[name] + k)[:, 0:dst.shape[1] if len(dst.shape) == 2 else SEQ]
                                ).then_inc(evac, 1)

            dve.memset(stage[:], 0.0).then_inc(stage_zero, 1)
            dve.memset(cin[:], 0.0).then_inc(f_taps, 1)
            dve.sem_inc(k_evac, 1)
            dve.memset(cc[:, 0:2, 0:1], 0.0).then_inc(f_gv, 2)
            dve.memset(cc[:, 2:4, 0:1], 0.0).then_inc(f_gl, 2)
            dve.wait_ge(in_par, 16 * 16)
            dve.tensor_copy(stage[0:2 * J, 6, :].rearrange("p (g q) -> p g q", g=2),
                            step_in[:].unsqueeze(2).to_broadcast([2 * J, 2, S5P])).then_inc(step_x, 1)
            take("params", 0, par[:, 0:4 * P])
            dve.wait_ge(filled, FILL["params"] + 2)
            dve.tensor_copy(par[:, 4 * P:7 * P], bank(T["params"] + 1)[:, 0:3 * P]).then_inc(evac, 1)
            dve.wait_ge(evac, 2)
            for m in range(KD):
                take("x", m, h[:, m, :])
                u_lo(0, m, uh0, ul0)
            rstd_of(0)
            lo_to(0)
            dve.wait_ge(unit_done, 1)
            lo_to(1)
            dve.tensor_tensor(dtT, bank(T["dt"])[0:2 * HEADS, :], rstd[0:2 * HEADS, :], ALU.mult).then_inc(evac, 1)
            count = [0]

            def sp_(op, *a, **k):
                if count[0]:
                    dve.wait_ge(sp_step, count[0])
                op(*a, **k).then_inc(sp_step, 1)
                count[0] += 1

            dve.wait_ge(dtx, 4)
            sp_(dve.tensor_scalar, spw, spz, 1.0, None, ALU.add)
            dve.wait_ge(dtx, 5)
            sp_(dve.tensor_scalar, spw, spw, -1.0, None, ALU.add)
            sp_(dve.tensor_scalar, speq, spw, 0.0, None, ALU.is_equal)
            sp_(dve.tensor_tensor, adT, adT, speq, ALU.add)
            sp_(dve.tensor_tensor, spw, spw, speq, ALU.add)
            sp_(dve.reciprocal, spw, spw)
            sp_(dve.tensor_tensor, adT, adT, spw, ALU.mult)
            sp_(dve.tensor_tensor, adT, adT, spz, ALU.mult)
            sp_(dve.scalar_tensor_tensor, out=dtT, in0=dtT, scalar=0.0, in1=adT, op0=ALU.max, op1=ALU.add)
            dve.wait_ge(sp_step, count[0])
            dve.tensor_scalar(adT, dtT, hvec[:, 2:3], -1.0, ALU.mult, ALU.mult).then_inc(adt, 1)
            dve.wait_ge(filled, FILL["seq"] + 1)
            s_t = bank(T["seq"]).rearrange("p (a c h) -> p a c h", a=2, c=SB)
            dve.tensor_copy(dt_seq[:], s_t[:, 0]).then_inc(adt, 1)
            dve.tensor_copy(ad_seq[:], s_t[:, 1]).then_inc(evac, 1)
            dve.wait_ge(filled, FILL["sums"] + 1)
            dve.tensor_copy(epq[:], bank(T["sums"]).rearrange("p (a c h) -> p a c h", a=2, c=SB)).then_inc(evac, 1)
            dve.wait_ge(filled, FILL["totals"] + 1)
            dve.tensor_copy(etot[:], bank(T["totals"])[:, 0:SB * 2 * HEADS].rearrange("p (c h) -> p c h", c=SB)
                            ).then_inc(evac, 1)
            dve.wait_ge(e_done, 2)
            dve.wait_ge(adt, 2)
            dve.tensor_tensor(epq[:, 1], epq[:, 1], dt_seq[:], ALU.mult).then_inc(eq_done, 1)
            dr = d_row[:].rearrange("p (t k) -> p t k", k=2)
            for k in range(2):
                dve.tensor_copy(d_col[64 * k:64 * k + 64, :], dr[64 * k:64 * k + 64, :, k]).then_inc(eq_done, 1)
            dve.wait_ge(eq_done, 3)

            for g in range(GROUPS):
                u = U[("ssd", g)]
                for i in range(3):
                    lo_to(u + 2 * i + 2)
                    pr = 3 * g + i
                    chans = [g * GT + 2 * i, g * GT + 2 * i + 1] if i < 2 else [INNER // P + g, INNER // P + GROUPS + g]
                    dve.wait_ge(unit_done, u + 2 * i + 2)
                    if pr >= 1:
                        dve.wait_ge(taps, 8 * pr)
                    for j in range(2):
                        dve.tensor_tensor(cin[:, j, 2:2 + SEQ], bank(T[("xbc", g)] + 2 * i + j), rstd[:], ALU.mult
                                          ).then_inc(evac, 1)
                    lo_to(u + 2 * i + 3)
                    for tap in range(1, 5):
                        for j in range(2):
                            q = 6 * g + 2 * i + j
                            if tap == 1:
                                dve.wait_ge(tap0, q + 1)
                            else:
                                dve.wait_ge(taps, 8 * pr + 2 * (tap - 1) + j - 1)
                            dve.scalar_tensor_tensor(
                                out=cc[:, q % 4, :], in0=cin[:, j, tap:tap + SEQ],
                                scalar=col(C_CONVW + tap * CONV_T + chans[j]), in1=cc[:, q % 4, :],
                                op0=ALU.mult, op1=ALU.add).then_inc(taps, 1)
                    lo_to(u + 2 * i + 4)
                for i in range(2):
                    lo_to(u + 6 + 2 * i + 2)
                    dve.wait_ge(unit_done, u + 6 + 2 * i + 2)
                    if g >= 1:
                        dve.wait_ge(yl_done, GT * g)
                    for j in range(2):
                        dve.tensor_tensor(zs[:, 2 * i + j, :], bank(T[("z", g)] + 2 * i + j), rstd[:], ALU.mult
                                          ).then_inc(evac, 1)
                    lo_to(min(u + 6 + 2 * i + 4, u + 11))
                for c in range(SB):
                    take(("xseq", g), c, xseq[:, c, :])
                dve.wait_ge(filled, FILL[("bseq", g)] + 1)
                dve.tensor_copy(bseq[:], bank(T[("bseq", g)]).rearrange("p (c n) -> p c n", c=SB)).then_inc(evac, 1)
                take(("cb", g), 0, cbT[:])
                chunks = [(0, 0), (1, SB - 1), (0, 1), (1, SB - 2), (0, 2), (1, SB - 3)]

                def heads(ap):
                    return ap.rearrange("p (h q) -> p h q", h=HPG)

                def per_head(ap):
                    return ap.unsqueeze(2).to_broadcast([P, HPG, HD])

                def hcols(d):
                    return slice(HEADS * d + HPG * g, HEADS * d + HPG * g + HPG)

                def decay_x(n):
                    d, c = chunks[n]
                    dve.wait_ge(evac, T[("xseq", g)] + c + 1)
                    if n >= 2:
                        dve.wait_ge(filled, FILL[("state", g)] + n - 1)
                    dve.tensor_tensor(heads(xd[:, n % 2, :]), heads(xseq[:, c, :]), per_head(epq[:, 1, c, hcols(d)]),
                                      ALU.mult).then_inc(xd_done, 1)

                decay_x(0)
                decay_x(1)
                for n in range(6):
                    d, c = chunks[n]
                    into = c if d == 0 else c - 1
                    if n >= 2:
                        prev = into - 1 if d == 0 else into + 1
                        dve.wait_ge(evac, T[("state", g)] + n - 1)
                        if n > 2:
                            dve.wait_ge(evac, T[("state", g)] + n)
                        dve.tensor_tensor(heads(ytmp[:]), heads(car[:, d, prev, :]), per_head(etot[:, c, hcols(d)]),
                                          ALU.mult).then_inc(car_mul, 1)
                        dve.wait_ge(car_mul, 4 * g + n - 1)
                        dve.wait_ge(filled, FILL[("state", g)] + n + 1)
                        dve.tensor_tensor(car[:, d, into, :], ytmp[:], bank(T[("state", g)] + n), ALU.add
                                          ).then_inc(evac, 1)
                    else:
                        take(("state", g), n, car[:, d, into, :])
                    if n + 2 < 6:
                        decay_x(n + 2)
                offs = [(0, 1), (1, 0), (0, 2), (1, 1), (0, 3), (1, 2)]
                dve.wait_ge(evac, T[("state", g)] + 6)
                adds = 0
                for n in range(6):
                    d, c = offs[n]
                    second = d == 1 and c > 0
                    dst = ytmp if second else yo[:, c, :]
                    dve.wait_ge(filled, FILL[("yoff", g)] + n + 1)
                    if second and adds:
                        dve.wait_ge(yo_add, 2 * g + adds)
                    dve.tensor_tensor(heads(dst[:] if second else dst), heads(bank(T[("yoff", g)] + n)),
                                      per_head(epq[:, 0, c, hcols(d)]), ALU.mult).then_inc(evac, 1)
                    if second:
                        dve.wait_ge(evac, T[("yoff", g)] + n + 1)
                        dve.tensor_tensor(yo[:, c, :], yo[:, c, :], ytmp[:], ALU.add).then_inc(yo_add, 1)
                        adds += 1

                def spread(ap, hp, d):
                    h0 = HEADS * d + HPG * g + 2 * hp
                    return ap[:, :, h0:h0 + 2].rearrange("p c h -> p h c").unsqueeze(3).to_broadcast([P, 2, SB, P])

                def mask(ap):
                    return ap[:].unsqueeze(1).unsqueeze(1).to_broadcast([P, 2, SB, P])

                def masked_logs(hp):
                    n = GT * g + hp
                    if n >= 1:
                        dve.wait_ge(e_full, n)
                    for d, m in ((0, le), (1, ge)):
                        dve.tensor_tensor(rr[:, d], spread(ad_seq, hp, d), mask(m), ALU.mult).then_inc(r_done, 1)

                def weights(hp):
                    n = GT * g + hp
                    if n >= 1:
                        dve.wait_ge(m_done, n)
                    for dst, d, m in ((wf, 0, le), (wb, 1, ge)):
                        dve.tensor_tensor(dst[:], spread(dt_seq, hp, d), mask(m), ALU.mult).then_inc(w_done, 1)
                    dve.wait_ge(w_done, 3 * n + 2)
                    dve.tensor_tensor(wf[:], wf[:], wb[:], ALU.add).then_inc(w_done, 1)

                def weigh(hp):
                    n = GT * g + hp
                    m = mm[:, n % 2]
                    dve.wait_ge(exp_done, n + 1)
                    dve.tensor_tensor(m, m, cbT[:].unsqueeze(1).to_broadcast([P, 2, SEQ]), ALU.mult).then_inc(m_half, 1)
                    dve.wait_ge(m_half, n + 1)
                    dve.wait_ge(w_done, 3 * n + 3)
                    dve.tensor_tensor(m, m, wf[:].rearrange("p h c l -> p h (c l)"), ALU.mult).then_inc(m_done, 1)

                def finish(hp):
                    n = GT * g + hp
                    dve.wait_ge(y_full, n + 1)
                    dve.scalar_tensor_tensor(out=xT[:, hp, :], in0=xT[:, hp, :], scalar=d_col[:, n:n + 1],
                                             in1=pe_y[:], op0=ALU.mult, op1=ALU.add).then_inc(y_skip, 1)
                    dve.wait_ge(y_skip, n + 1)
                    dve.wait_ge(z_silu, n + 1)
                    dve.tensor_tensor(xT[:, hp, :], xT[:, hp, :], zs[:, hp, :], ALU.mult).then_inc(gated, 1)

                masked_logs(0)
                for hp in range(HPG // 2):
                    weights(hp)
                    if hp + 1 < HPG // 2:
                        masked_logs(hp + 1)
                    weigh(hp)
                    if hp:
                        finish(hp - 1)
                finish(HPG // 2 - 1)
                dve.wait_ge(gsq_used, GT * g + GT)
                dve.tensor_scalar(var[:], pe_s[:], 1.0 / GC, EPS, ALU.mult, ALU.add).then_inc(gvar, 1)
                dve.wait_ge(gstd, g + 1)
                dve.reciprocal(ytmp[:], var[:]).then_inc(grstd, 1)
                dve.wait_ge(grstd, g + 1)
                for m in range(GT):
                    dve.wait_ge(gated, GT * g + m + 1)
                    dve.scalar_tensor_tensor(out=zs[:, m, :], in0=xT[:, m, :], scalar=col(C_SSDN + GT * g + m),
                                             in1=ytmp[:], op0=ALU.mult, op1=ALU.mult).then_inc(yn_done, 1)
                for m in range(GT):
                    dve.wait_ge(yh_done, GT * g + m + 1)
                    dve.tensor_tensor(yl[:, m, :], zs[:, m, :], yh[:, m, :].bitcast(F32), ALU.subtract
                                      ).then_inc(yl_done, 1)
                for i in range(4):
                    lo_to(u + 10 + i + 1)
                    dve.wait_ge(unit_done, u + 10 + i + 1)
                    for m in (2 * i, 2 * i + 1):
                        if g:
                            dve.wait_ge(evac, T[("out", g - 1)] + m + 1)
                        dve.tensor_tensor(h[:, m, :], h[:, m, :], bank(T[("out", g)] + m), ALU.add).then_inc(evac, 1)
                    lo_to(u + 10 + i + 2)
                    if g == GROUPS - 1:
                        for m in (2 * i, 2 * i + 1):
                            u_lo(1, m, uh0, ul0)

            for layer in range(2):
                gh, gl, p_in, ph, pl, pproj = FFN[layer]
                if layer == 1:
                    rstd_of(3)
                    for m in range(KD):
                        dve.scalar_tensor_tensor(out=u5[:, m, :], in0=h[:, m, :], scalar=col(NORM_COL[3] + m),
                                                 in1=rstd[:], op0=ALU.mult, op1=ALU.mult).then_inc(u5_done, 1)
                    for n in range(8):
                        dve.wait_ge(filled, FILL["c5"] + n + 1)
                        src = bank(T["c5"] + n).rearrange("p (b j g q) -> p b j g q", b=4, j=BP, g=2)
                        for g in range(2):
                            rows = slice(64 * g, 64 * g + 64)
                            dve.tensor_copy(cst[rows, n // 2, 4 * (n % 2):4 * (n % 2) + 4, :, :],
                                            src[rows, :, :, g, :]).then_inc((c5_half, evac)[g], 1)

                    lr = par[:, C_A:C_A + 2 * J]
                    li = par[:, C_A + 2 * J:C_A + 4 * J]
                    step, mag, sin, half, n_, ang, lam_r, lam_i, q_r, q_i, cos, s_a, s_b, s_c, s_d, mag4 = (
                        v5[:, i, :] for i in range(16))
                    count = [0]

                    def v(op, *a, **k):
                        if count[0]:
                            dve.wait_ge(v_dve, count[0])
                        op(*a, **k).then_inc(v_dve, 1)
                        count[0] += 1

                    def tt(o, a, b, f):
                        v(dve.tensor_tensor, o, a, b, f)

                    dve.wait_ge(v_act, 1)
                    tt(mag, lr, step, ALU.mult)
                    tt(ang, li, step, ALU.mult)
                    v(dve.tensor_scalar, n_, ang, 1.0 / (2.0 * PI), ROUND_MAGIC, ALU.mult, ALU.add)
                    v(dve.tensor_scalar, n_, n_, -ROUND_MAGIC, None, ALU.add)
                    for part_ in (TWO_PI_HI, TWO_PI_MID, TWO_PI_LO):
                        v(dve.scalar_tensor_tensor, out=ang, in0=n_, scalar=-part_, in1=ang, op0=ALU.mult,
                          op1=ALU.add)
                    v(dve.tensor_scalar, ang, ang, PI_BELOW, -PI_BELOW, ALU.min, ALU.max)
                    dve.wait_ge(v_act, 4)
                    tt(half, half, half, ALU.mult)
                    v(dve.tensor_scalar, cos, half, -2.0, 1.0, ALU.mult, ALU.add)
                    tt(lam_r, mag, cos, ALU.mult)
                    tt(lam_i, mag, sin, ALU.mult)
                    v(dve.tensor_scalar, s_a, lam_r, -1.0, None, ALU.add)
                    tt(s_b, lr, lr, ALU.mult)
                    tt(s_c, li, li, ALU.mult)
                    tt(s_b, s_b, s_c, ALU.add)
                    v(dve.reciprocal, s_b, s_b)
                    tt(s_c, s_a, lr, ALU.mult)
                    tt(s_d, lam_i, li, ALU.mult)
                    tt(s_c, s_c, s_d, ALU.add)
                    tt(q_r, s_c, s_b, ALU.mult)
                    tt(s_c, lam_i, lr, ALU.mult)
                    tt(s_d, s_a, li, ALU.mult)
                    tt(s_c, s_c, s_d, ALU.subtract)
                    tt(q_i, s_c, s_b, ALU.mult)
                    tt(s_a, mag, mag, ALU.mult)
                    tt(mag4, s_a, s_a, ALU.mult)
                    tt(s_a, cos, cos, ALU.mult)
                    tt(s_b, sin, sin, ALU.mult)
                    v(dve.scalar_tensor_tensor, out=s_c, in0=cos, scalar=2.0, in1=sin, op0=ALU.mult, op1=ALU.mult)
                    tt(s_d, s_a, s_b, ALU.subtract)
                    tt(s_a, s_d, s_d, ALU.mult)
                    tt(s_b, s_c, s_c, ALU.mult)
                    tt(cos, s_a, s_b, ALU.subtract)
                    v(dve.scalar_tensor_tensor, out=sin, in0=s_c, scalar=2.0, in1=s_d, op0=ALU.mult, op1=ALU.mult)

                    def by_block(a):
                        return a.rearrange("p (d b j) -> p d b j", d=2, b=NB)

                    def in_blocks(a):
                        return a.rearrange("p (b d j) -> p d b j", d=2, b=NB)

                    for d, sign in ((0, 1.0), (1, -1.0)):
                        v(dve.tensor_copy, in_blocks(tn[:, 0, 0, :])[:, d], by_block(cos)[:, d])
                        v(dve.tensor_scalar, in_blocks(tn[:, 1, 0, :])[:, d], by_block(sin)[:, d], sign, None, ALU.mult)
                        v(dve.tensor_copy, in_blocks(m4v[:])[:, d], by_block(mag4)[:, d])
                        for kind in range(2):
                            for a, lam in ((0, lam_r), (1, lam_i)):
                                v(dve.tensor_copy, lamx[:, a, :, (2 * kind + d) * BP:(2 * kind + d + 1) * BP],
                                  by_block(lam)[:, d])
                    for n in range(1, 7):
                        tt(s_a, tn[:, 0, n - 1, :], tn[:, 0, n - 1, :], ALU.mult)
                        tt(s_b, tn[:, 1, n - 1, :], tn[:, 1, n - 1, :], ALU.mult)
                        tt(tn[:, 0, n, :], s_a, s_b, ALU.subtract)
                        v(dve.scalar_tensor_tensor, out=tn[:, 1, n, :], in0=tn[:, 0, n - 1, :], scalar=2.0,
                          in1=tn[:, 1, n - 1, :], op0=ALU.mult, op1=ALU.mult)
                    v(dve.memset, rot[:, 0, :, 0:1], 1.0)
                    v(dve.memset, rot[:, 1, :, 0:1], 0.0)
                    dve.wait_ge(evac, T["c5"] + 8)
                    dve.wait_ge(c5_half, 8)
                    prod = [t[:].rearrange("p (a x) k -> p a (x k)", a=2).rearrange(
                        "p a (j q) -> p a j q", q=S5H) for t in (ta, tb)]
                    c_all = cst.rearrange("p (a d) b j q -> p d a (b j) q", a=2)
                    for d in range(2):
                        for a in range(2):
                            for pr_, qv in ((prod[0], q_r), (prod[1], q_i)):
                                tt(pr_[:, a], c_all[:, d, a],
                                   qv[:, d * J:(d + 1) * J].unsqueeze(2).to_broadcast([P, J, S5H]), ALU.mult)
                        tt(cw[:, 0, d], prod[0][:, 0], prod[1][:, 1], ALU.subtract)
                        tt(cw[:, 1, d], prod[0][:, 1], prod[1][:, 0], ALU.add)
                    dve.wait_ge(v_dve, count[0])
                    dve.drain().then_inc(cw_done, 1)

                    dirs = "p (d j) k -> p d (j k)"
                    t0, f0 = T["s5"], FILL["s5"]
                    e_re, e_im = ring[:, (t0 + 4) % 4:(t0 + 4) % 4 + 2, :], ring[:, (t0 + 6) % 4:(t0 + 6) % 4 + 2, :]
                    c_, s_ = (rot[:, a].rearrange(dirs, d=2) for a in range(2))
                    z_ = [zz[:, a].rearrange(dirs, d=2) for a in range(2)]
                    a_, b_ = ta[:].rearrange(dirs, d=2), tb[:].rearrange(dirs, d=2)
                    m_ = m4[:].rearrange(dirs, d=2)
                    with dve.Fori(0, NB) as b:
                        dve.wait_ge(pw0, b * 8 + 8)
                        lam = [lamx[:, a, bass.ds(b, 1), :].rearrange("p b q -> p (b q)").unsqueeze(1).unsqueeze(3)
                               .to_broadcast([P, 2, 4 * BP, S5H]) for a in range(2)]
                        for tau in range(TAU):
                            now = pw[:, tau].rearrange("p a q j h -> p a (q j) h")
                            then = pw[:, tau + 1].rearrange("p a q j h -> p a (q j) h")
                            if tau:
                                dve.wait_ge(pw_r, b * (2 * TAU) + 2 * tau)
                            dve.tensor_tensor(px[:], now, lam[0], ALU.mult).then_inc(pw_x, 1)
                            dve.tensor_tensor(py[:], now, lam[1], ALU.mult).then_inc(pw_x, 1)
                            dve.wait_ge(pw_x, b * (2 * TAU) + 2 * tau + 2)
                            dve.tensor_tensor(then[:, 0], px[:, 0], py[:, 1], ALU.subtract).then_inc(pw_r, 1)
                            dve.tensor_tensor(then[:, 1], px[:, 1], py[:, 0], ALU.add).then_inc(pw_r, 1)
                        for n in range(7):
                            w = 1 << n
                            turn = [tn[:, a, n, bass.ds(b * 8, 8)].unsqueeze(1).unsqueeze(3)
                                    .to_broadcast([P, 2, 2 * BP, w]) for a in range(2)]
                            tx = [t[:].rearrange("p (a x) k -> p a (x k)", a=2)[:, :, 0:2 * BP * w].rearrange(
                                "p a (q k) -> p a q k", k=w) for t in (ta, tb)]
                            if n:
                                dve.wait_ge(rot_r, b * 14 + 2 * n)
                            for x_, tr in zip(tx, turn):
                                dve.tensor_tensor(x_, rot[:, :, :, 0:w], tr, ALU.mult).then_inc(rot_x, 1)
                            dve.wait_ge(rot_x, b * 14 + 2 * n + 2)
                            dve.tensor_tensor(rot[:, 0, :, w:2 * w], tx[0][:, 0], tx[1][:, 1], ALU.subtract
                                              ).then_inc(rot_r, 1)
                            dve.tensor_tensor(rot[:, 1, :, w:2 * w], tx[0][:, 1], tx[1][:, 0], ALU.add
                                              ).then_inc(rot_r, 1)
                        dve.wait_ge(s5_zero, 6)
                        dve.tensor_tensor(
                            m4[:].rearrange("p (d j) k -> p d j k", d=2),
                            m4v[:, bass.ds(b * 8, 8)].rearrange("p (d j) -> p d j", d=2).unsqueeze(3)
                            .to_broadcast([P, 2, BP, NCH]),
                            smask[:].unsqueeze(2).to_broadcast([P, 2, BP, NCH]), ALU.mult).then_inc(m4_r, 1)
                        for n in range(4):
                            dve.wait_ge(filled, b * 8 + (f0 + n + 1))
                            dve.tensor_copy(vT[:, n // 2, n % 2].rearrange("p j q -> p (j q)"), bank(t0 + n)
                                            ).then_inc(evac, 1)
                        dve.wait_ge(k_full, b + 1)
                        dve.tensor_copy(kT[:].rearrange("p j q -> p (j q)"), pe_e[:, 0, :]).then_inc(k_evac, 1)
                        dve.wait_ge(filled, b * 8 + (f0 + 8))
                        dve.wait_ge(rot_r, b * 14 + 14)
                        dve.tensor_tensor(a_, e_re, c_, ALU.mult).then_inc(spin, 1)
                        dve.tensor_tensor(b_, e_im, s_, ALU.mult).then_inc(spin, 1)
                        dve.wait_ge(spin, b * 8 + 2)
                        dve.tensor_tensor(z_[0], a_, b_, ALU.add).then_inc(spin, 1)
                        dve.wait_ge(spin, b * 8 + 3)
                        dve.tensor_tensor(a_, e_im, c_, ALU.mult).then_inc(spin, 1)
                        dve.tensor_tensor(b_, e_re, s_, ALU.mult).then_inc(evac, 4)
                        dve.wait_ge(spin, b * 8 + 4)
                        dve.wait_ge(evac, b * 8 + (t0 + 8))
                        dve.tensor_tensor(z_[1], a_, b_, ALU.subtract).then_inc(spin, 1)
                        dve.wait_ge(spin, b * 8 + 5)
                        dve.wait_ge(m4_r, b + 1)
                        for z1, o1 in zip(z_, (a_, b_)):
                            for d in range(2):
                                r = slice(None, None, (1, -1)[d])
                                dve.tensor_tensor_scan(o1[:, d][:, r], m_[:, d][:, r], z1[:, d][:, r], 0.0,
                                                       ALU.mult, ALU.add).then_inc(scan, 1)
                        dve.wait_ge(scan, b * 4 + 4)
                        dve.tensor_tensor(z_[0], a_, c_, ALU.mult).then_inc(spin, 1)
                        dve.tensor_tensor(z_[1], b_, s_, ALU.mult).then_inc(spin, 1)
                        dve.wait_ge(spin, b * 8 + 7)
                        dve.wait_ge(y5_full, b + 1)
                        kk = "p (j k) -> p j k"
                        for d in range(2):
                            dve.tensor_tensor(xs[:, 0, d, :, 1 - d:1 - d + NCH], z_[0][:, d].rearrange(kk, j=BP),
                                              z_[1][:, d].rearrange(kk, j=BP), ALU.subtract).then_inc(xs_r, 1)
                        dve.wait_ge(xs_r, b * 4 + 2)
                        dve.tensor_tensor(z_[0], b_, c_, ALU.mult).then_inc(spin, 1)
                        dve.tensor_tensor(z_[1], a_, s_, ALU.mult).then_inc(zz_r, 1)
                        dve.wait_ge(spin, b * 8 + 8)
                        dve.wait_ge(zz_r, b + 1)
                        for d in range(2):
                            dve.tensor_tensor(xs[:, 1, d, :, 1 - d:1 - d + NCH], z_[0][:, d].rearrange(kk, j=BP),
                                              z_[1][:, d].rearrange(kk, j=BP), ALU.add).then_inc(xs_r, 1)
                        dve.wait_ge(y5_un, b * 16 + 16)
                        dve.wait_ge(xs_r, b * 4 + 4)
                        dve.scalar_tensor_tensor(out=y5[:], in0=u5[:, bass.ds(b, 1), :].rearrange("p b t -> p (b t)"),
                                                 scalar=dcol(b + C_S5D), in1=y5[:], op0=ALU.mult, op1=ALU.add
                                                 ).then_inc(y5_skip, 1)
                    for m in range(KD):
                        dve.wait_ge(g5_hi, m + 1)
                        dve.tensor_tensor(gl5[:, m, :], u5[:, m, :], gh5[:, m, :].bitcast(F32), ALU.subtract
                                          ).then_inc(g5_lo, 1)
                    u, t = U["glu"], T["glu"]
                    for i in range(4):
                        for half in range(2):
                            lo_to(u + 4 * i + 2 * half + 2)
                            dve.wait_ge(unit_done, u + 4 * i + 2 * half + 2)
                            if i:
                                dve.wait_ge(h_upd, KD + 2 * i)
                            for j in range(2):
                                dve.tensor_scalar(cc[:, 2 * half + j, :], bank(t + 4 * i + 2 * half + j),
                                                  col(C_BGLU + half * KD + 2 * i + j), None, ALU.add
                                                  ).then_inc(evac, 1)
                            lo_to(u + 4 * i + 2 * half + 3)
                        for j in range(2):
                            dve.wait_ge(glu_sig, 2 * i + j + 1)
                            dve.tensor_tensor(cc[:, j, :], cc[:, j, :], cc[:, 2 + j, :], ALU.mult).then_inc(glu_mul, 1)
                        for j in range(2):
                            dve.wait_ge(glu_mul, 2 * i + j + 1)
                            dve.tensor_tensor(h[:, 2 * i + j, :], h[:, 2 * i + j, :], cc[:, j, :], ALU.add
                                              ).then_inc(h_upd, 1)
                        for m in (2 * i, 2 * i + 1):
                            u_lo(4, m, uh1, ul1)
                rstd_of(1 + 3 * layer)
                u, t = U[("up", layer)], T[("up", layer)]
                lo_to(u + 2)
                done = layer * HT
                with dve.Fori(0, PAIRS) as i:
                    for half in range(2):
                        dve.wait_ge(unit_done, i * 4 + (u + 2 * half + 2))
                        dve.wait_ge(f_taps, i * 8 + (4 * done + 4 * half + 1))
                        for j in range(2):
                            dve.tensor_tensor(cin[:, j, 2:2 + SEQ], bank(t + 2 * half + j), rstd[:], ALU.mult
                                              ).then_inc(evac, 1)
                        lo(u + 2 * half + 3, at=i * 4)
                        for tap in range(1, 3):
                            for j in range(2):
                                if tap == 1:
                                    dve.wait_ge(f_c0, i * 4 + (2 * done + 2 * half + j + 1))
                                else:
                                    dve.wait_ge(f_taps, i * 8 + (4 * done + 4 * half + j + 2))
                                c = 2 * HT * (3 * layer + tap) + half * HT + j
                                dve.scalar_tensor_tensor(out=cc[:, 2 * half + j, :], in0=cin[:, j, 1 + tap:1 + tap + SEQ],
                                                         scalar=dcol(i * 2 + (C_FCW + c)), in1=cc[:, 2 * half + j, :],
                                                         op0=ALU.mult, op1=ALU.add).then_inc(f_taps, 1)
                        if half == 0:
                            lo(u + 4, at=i * 4)
                    for j in range(2):
                        dve.wait_ge(f_silu, i * 2 + (done + j + 1))
                        dve.wait_ge(f_taps, i * 8 + (4 * done + 6 + j + 2))
                        dve.tensor_tensor(cc[:, 2 + j, :], cc[:, j, :], cc[:, 2 + j, :], ALU.mult).then_inc(f_gv, 1)
                    lo(u + 6, at=i * 4)
                    for j in range(2):
                        dve.wait_ge(f_gh, i * 2 + (done + j + 1))
                        dve.tensor_tensor(gl[:, bass.ds(i * 2 + j, 1), :].rearrange("p a t -> p (a t)"), cc[:, 2 + j, :],
                                          gh[:, bass.ds(i * 2 + j, 1), :].rearrange("p a t -> p (a t)").bitcast(F32),
                                          ALU.subtract).then_inc(f_gl, 1)
                split[0] = U[("down", layer)] + 2
                dve.wait_ge(f_gv, HT * (layer + 1) + 2)
                for k in range(PK):
                    take(("p", layer), k, cc[:, k, :])
                for k in range(PK):
                    dve.wait_ge(p_hi, PK * layer + k + 1)
                    dve.tensor_tensor(pl[:, k, :], cc[:, k, :], ph[:, k, :].bitcast(F32), ALU.subtract).then_inc(p_lo, 1)
                u, t = U[("down", layer)], T[("down", layer)]
                r = 2 + 3 * layer
                for i in range(4):
                    lo_to(u + 6 * i + 6)
                    dve.wait_ge(unit_done, u + 6 * i + 6)
                    for m in (2 * i, 2 * i + 1):
                        dve.tensor_tensor(h[:, m, :], h[:, m, :], bank(t + m), ALU.add).then_inc(evac, 1)
                    lo_to(u + 6 * i + 7)
                    for m in (2 * i, 2 * i + 1):
                        u_lo(r, m, UH[layer], UL[layer])
                rstd_of(r)
                for i in range(2):
                    lo_to(U[("proj", layer)] + i + 1)
                    dve.wait_ge(unit_done, U[("proj", layer)] + i + 1)
                    for m in range(4 * i, 4 * i + 4):
                        dve.tensor_copy(pproj[:, m, :], bank(T[("proj", layer)] + m)).then_inc(evac, 1)
                    lo_to(U[("proj", layer)] + i + 2)
                u, t = U[("gate", layer)], T[("gate", layer)]
                before = 2 * KD * layer
                for i in range(4):
                    lo_to(u + 2 * i + 2)
                    dve.wait_ge(unit_done, u + 2 * i + 2)
                    if i >= 2:
                        dve.wait_ge(h_upd, before + 2 * i - 2)
                    if i == 0:
                        dve.wait_ge(p_lo, PK * (layer + 1))
                    for m in (2 * i, 2 * i + 1):
                        dve.tensor_tensor(cc[:, m % 4, :], bank(t + m), rstd[:], ALU.mult).then_inc(evac, 1)
                    lo_to(u + 2 * i + 3)
                    for m in (2 * i, 2 * i + 1):
                        dve.wait_ge(g_sig, KD * layer + m + 1)
                        dve.tensor_tensor(cc[:, m % 4, :], cc[:, m % 4, :], pproj[:, m, :], ALU.mult).then_inc(g_mul, 1)
                    lo_to(min(u + 2 * i + 4, u + 9))
                    for m in (2 * i, 2 * i + 1):
                        dve.wait_ge(g_mul, KD * layer + m + 1)
                        dve.tensor_tensor(h[:, m, :], h[:, m, :], cc[:, m % 4, :], ALU.add).then_inc(h_upd, 1)

            rstd_of(6)
            for m in range(KD):
                dve.wait_ge(*h_ready(6, m))
                dve.scalar_tensor_tensor(out=hn[:, m, :], in0=h[:, m, :], scalar=col(NORM_COL[6] + m), in1=rstd[:],
                                         op0=ALU.mult, op1=ALU.mult).then_inc(hn_done, 1)
            for b in range(SB):
                for half in range(2):
                    take("final", 2 * b + half, o_sb[:, b, half * SEQ:(half + 1) * SEQ])

        @block.tensor
        def _(pe):
            def product(u, t, nk, k0, rh, rl, at=0, tiles=2, width=P, first=True, last=True):
                pe.wait_ge(lo_done, at + (u + 1))
                if first:
                    pe.wait_ge(evac, at + (t + tiles - 4))
                wh, wl = part(w_hi, u, nk), part(w_lo, u, nk)
                for j in range(tiles):
                    o = bank(t + j)[0:width, :]
                    for k in range(nk):
                        c = slice(j * width, j * width + width)
                        pe.matmul(o, wh[:, k, c], rh[:, k0 + k, :], start=first and k == 0, stop=False)
                        pe.matmul(o, wh[:, k, c], rl[:, k0 + k, :], start=False, stop=False)
                        mm_ = pe.matmul(o, wl[:, k, c], rh[:, k0 + k, :], start=False, stop=last and k == nk - 1)
                mm_.then_inc(unit_done, 1)

            def add_square(r, m):
                pe.wait_ge(sq_done, KD * r + m + 1)
                if m == 0 and r == 1:
                    pe.wait_ge(gvar, GROUPS)
                elif m == 0 and r > 1:
                    pe.wait_ge(var_done, r)
                pe.matmul(pe_s[:], ones[:], sq[:, m % 2, :], start=m == 0, stop=m == KD - 1).then_inc(sq_used, 1)

            pe.wait_ge(masks, 11)
            pe.wait_ge(in_par, 16 * 16)
            pe.wait_ge(step_x, 1)
            for i in range(7):
                mm_ = pe.transpose(bank(T["params"] + i // 4)[:, (i % 4) * P:(i % 4 + 1) * P], stage[:, i, :], eye[:])
                if i in (3, 6):
                    mm_.then_inc(filled, 1)
            pe.wait_ge(in_x, 16)
            for m in range(KD):
                if T["x"] + m >= 4:
                    pe.wait_ge(evac, T["x"] + m - 3)
                for b in range(SB):
                    mm_ = pe.transpose(bank(T["x"] + m)[:, b * P:(b + 1) * P], x_in[:, b, m * P:(m + 1) * P], eye[:])
                mm_.then_inc(filled, 1)
                if m:
                    add_square(0, m - 1)
            add_square(0, KD - 1)
            pe.wait_ge(ul_done, KD)
            product(U["dt"], T["dt"], KD, 0, uh0, ul0, tiles=1, width=2 * HEADS)
            pe.wait_ge(evac, T["seq"] - 3)
            pe.wait_ge(adt, 1)
            s_t = bank(T["seq"]).rearrange("p (a c q) -> p a c q", a=2, c=SB)
            for a, src in enumerate((dtT, adT)):
                for c in range(SB):
                    mm_ = pe.transpose(s_t[:, a, c, :], src[:, c * P:(c + 1) * P], eye[0:2 * HEADS, 0:2 * HEADS])
            mm_.then_inc(filled, 1)
            pe.wait_ge(evac, T["sums"])
            s_t = bank(T["sums"]).rearrange("p (a c q) -> p a c q", a=2, c=SB)
            for a, d, m in ((0, 0, le), (0, 1, ge), (1, 0, gt), (1, 1, lt)):
                q = slice(HEADS * d, HEADS * d + HEADS)
                mm_ = pe.matmul(s_t[:, a, :, q], m[:], ad_seq[:, :, q], start=True, stop=True)
            mm_.then_inc(filled, 1)
            pe.wait_ge(evac, T["totals"] - 3)
            pe.matmul(bank(T["totals"])[:, 0:SB * 2 * HEADS], ones[:], ad_seq[:].rearrange("p c q -> p (c q)"),
                      start=True, stop=True).then_inc(filled, 1)

            for g in range(GROUPS):
                u = U[("ssd", g)]
                for i in range(3):
                    for kg in range(2):
                        product(u + 2 * i + kg, T[("xbc", g)] + 2 * i, 4, 4 * kg, uh0, ul0, first=kg == 0, last=kg == 1)
                for i in range(2):
                    for kg in range(2):
                        product(u + 6 + 2 * i + kg, T[("z", g)] + 2 * i, 4, 4 * kg, uh0, ul0, first=kg == 0,
                                last=kg == 1)
                pe.wait_ge(silu, 6 * g + 6)
                for c in range(SB):
                    ck = slice(c * P, c * P + P)
                    pe.wait_ge(evac, T[("xseq", g)] + c - 3)
                    for i in range(GT):
                        mm_ = pe.transpose(bank(T[("xseq", g)] + c)[:, i * P:(i + 1) * P], xT[:, i, ck], eye[:])
                    mm_.then_inc(filled, 1)
                pe.wait_ge(evac, T[("bseq", g)] - 3)
                for c in range(SB):
                    ck = slice(c * P, c * P + P)
                    mm_ = pe.transpose(bank(T[("bseq", g)])[:, ck], bT[:, ck], eye[:])
                mm_.then_inc(filled, 1)
                pe.wait_ge(evac, T[("cb", g)] - 3)
                for c in range(SB):
                    ck = slice(c * P, c * P + P)
                    mm_ = pe.matmul(bank(T[("cb", g)])[:, ck], bT[:, ck], cT[:, ck], start=True, stop=True)
                mm_.then_inc(filled, 1)
                pe.wait_ge(evac, T[("bseq", g)] + 1)
                for n, (d, c) in enumerate([(0, 0), (1, SB - 1), (0, 1), (1, SB - 2), (0, 2), (1, SB - 3)]):
                    pe.wait_ge(xd_done, 6 * g + n + 1)
                    pe.wait_ge(evac, T[("state", g)] + n - 3)
                    pe.matmul(bank(T[("state", g)] + n), bseq[:, c, :], xd[:, n % 2, :], start=True, stop=True
                              ).then_inc(filled, 1)
                for n, (d, c) in enumerate([(0, 1), (1, 0), (0, 2), (1, 1), (0, 3), (1, 2)]):
                    if n == 0:
                        pe.wait_ge(evac, T[("state", g)] + 6)
                    else:
                        pe.wait_ge(evac, T[("yoff", g)] + n - 3)
                    pe.matmul(bank(T[("yoff", g)] + n), cT[:, c * P:(c + 1) * P], car[:, d, c - 1 if d == 0 else c, :],
                              start=True, stop=True).then_inc(filled, 1)

                def exponents(hp):
                    n = GT * g + hp
                    pe.wait_ge(r_done, 2 * n + 2)
                    if n:
                        pe.wait_ge(exp_done, n)
                    for k in range(2):
                        pe.matmul(pe_e[:, k, :], gt[:], rr[:, 0, k].rearrange("p c l -> p (c l)"), start=True, stop=False)
                        mm_ = pe.matmul(pe_e[:, k, :], lt[:], rr[:, 1, k].rearrange("p c l -> p (c l)"), start=False,
                                        stop=True)
                    mm_.then_inc(e_full, 1)

                def outputs(hp):
                    n = GT * g + hp
                    if n:
                        pe.wait_ge(y_skip, n)
                    if hp == 0:
                        pe.wait_ge(evac, T[("yoff", g)] + 6)
                        pe.wait_ge(yo_add, 2 * g + 2)
                    for c in range(SB):
                        pe.matmul(pe_y[:, c * P:(c + 1) * P], yo[:, c, hp * P:(hp + 1) * P], eye[:], start=c == 0,
                                  stop=False, skip_group_check=True)
                    pe.wait_ge(m_done, n + 1)
                    for k in range(2):
                        for c in range(SB):
                            mm_ = pe.matmul(pe_y[64 * k:64 * k + 64, c * P:(c + 1) * P],
                                            xseq[:, c, (2 * hp + k) * HD:(2 * hp + k + 1) * HD],
                                            mm[:, n % 2, k, c * P:(c + 1) * P], start=False,
                                            stop=True, skip_group_check=True)
                    mm_.then_inc(y_full, 1)

                def group_square(hp):
                    n = GT * g + hp
                    pe.wait_ge(gsq, n + 1)
                    if hp == 0:
                        pe.wait_ge(*((gvar, g) if g else (var_done, 1)))
                    pe.matmul(pe_s[:], ones[:], sq[:, n % 2, :], start=hp == 0, stop=hp == GT - 1).then_inc(gsq_used, 1)

                exponents(0)
                for hp in range(GT):
                    if hp + 1 < GT:
                        exponents(hp + 1)
                    outputs(hp)
                    if hp:
                        group_square(hp - 1)
                group_square(GT - 1)
                for i in range(4):
                    if i == 0:
                        pe.wait_ge(yl_done, GT * g + GT)
                    product(u + 10 + i, T[("out", g)] + 2 * i, GT, 0, yh, yl)
                    if g == GROUPS - 1 and i:
                        add_square(1, 2 * i - 2)
                        add_square(1, 2 * i - 1)

            for layer in range(2):
                gh, gl, p_in, ph, pl, pproj = FFN[layer]
                uh, ul = UH[layer], UL[layer]
                r = 1 + 3 * layer
                if layer == 1:
                    pe.wait_ge(c_loaded, 16 * 8)
                    for n in range(8):
                        pe.wait_ge(evac, T["c5"] + n - 3)
                        for k in range(4):
                            mm_ = pe.transpose(bank(T["c5"] + n)[:, k * P:(k + 1) * P],
                                               c_in[:, n // 2, 4 * (n % 2) + k, :], eye[:])
                        mm_.then_inc(filled, 1)
                    pe.sem_inc(y5_full, 1)
                    t0 = T["s5"]
                    with pe.Fori(0, NB) as b:
                        pe.wait_ge(blk, b * 16 + 17)
                        for n in range(4):
                            pe.wait_ge(evac, b * 8 + (t0 + n - 3))
                            for j in range(BP):
                                mm_ = pe.transpose(bank(t0 + n)[:, j * P:(j + 1) * P],
                                                   vblk[:, n // 2, n % 2, j].rearrange("p t q -> p (t q)"), eye[:])
                            mm_.then_inc(filled, 1)
                        pe.wait_ge(k_evac, b + 1)
                        for j in range(BP):
                            for s in range(TAU):
                                o = pe_e[CH * s:CH * s + CH, 0, j * P:(j + 1) * P]
                                for d in range(2):
                                    for a in range(2):
                                        b_in = vblk[:, a, 1, j, 0, :]
                                        if d == 0:
                                            c_out, oo = cblk[:, a, 0, j, 0:TAU - s, :], o[:, CH * s:]
                                        else:
                                            c_out, oo = cblk[:, a, 1, j, TAU - s:TAU + 1, :], o[:, 0:CH * (s + 1)]
                                        mm_ = pe.matmul(oo, b_in, c_out.rearrange("p t q -> p (t q)"),
                                                        start=(j, d, a) == (0, 0, 0), stop=(j, d, a) == (BP - 1, 1, 1),
                                                        skip_group_check=True)
                        mm_.then_inc(k_full, 1)
                        pe.wait_ge(lift, b * 16 + 16)
                        for n in range(4):
                            pe.wait_ge(evac, b * 8 + (t0 + 4 + n - 3))
                            for j in range(BP):
                                mm_ = pe.matmul(bank(t0 + 4 + n)[:, j * P:(j + 1) * P], vT[:, n // 2, n % 2, j, :],
                                                ulift[:, j, :], start=True, stop=True)
                            mm_.then_inc(filled, 1)
                        pe.wait_ge(k_evac, b + 2)
                        pe.wait_ge(xs_r, b * 4 + 4)
                        for j in range(BP):
                            o = pe_y[:, j * NCH:(j + 1) * NCH]
                            pe.matmul(o, kT[:, j, :], ulift[:, j, :], start=j == 0, stop=False, skip_group_check=True)
                            for a in range(2):
                                pe.matmul(o, cblk[:, a, 0, j, 1:TAU + 1, :].rearrange("p t q -> p (t q)"),
                                          xs[:, a, 0, j, 0:NCH], start=False, stop=False, skip_group_check=True)
                                mm_ = pe.matmul(o, cblk[:, a, 1, j, 0:TAU, :].rearrange("p t q -> p (t q)"),
                                                xs[:, a, 1, j, 1:NCH + 1], start=False, stop=a == 1,
                                                skip_group_check=True)
                        mm_.then_inc(y5_full, 1)
                    u, t = U["glu"], T["glu"]
                    for i in range(4):
                        for half in range(2):
                            for kg in range(2):
                                if i == 0 and half == 0:
                                    pe.wait_ge(g5_lo, 4 * kg + 4)
                                product(u + 4 * i + 2 * half + kg, t + 4 * i + 2 * half, 4, 4 * kg, gh5, gl5,
                                        first=kg == 0, last=kg == 1)
                        if i:
                            add_square(4, 2 * i - 2)
                            add_square(4, 2 * i - 1)
                add_square(r, KD - 2)
                add_square(r, KD - 1)
                u, t = U[("up", layer)], T[("up", layer)]
                with pe.Fori(0, PAIRS) as i:
                    for half in range(2):
                        for kg in range(2):
                            if half == 0:
                                pe.wait_ge(ul_done, KD * SPLIT[r] + 4 * kg + 4)
                            product(u + 2 * half + kg, t + 2 * half, 4, 4 * kg, uh, ul, at=i * 4, first=kg == 0,
                                    last=kg == 1)
                pe.wait_ge(p_loaded[layer], 16)
                for k in range(PK):
                    pe.wait_ge(evac, T[("p", layer)] + k - 3)
                    for b in range(SB):
                        mm_ = pe.transpose(bank(T[("p", layer)] + k)[:, b * P:(b + 1) * P],
                                           p_in[:, b, k * P:(k + 1) * P], eye[:])
                    mm_.then_inc(filled, 1)
                u, t = U[("down", layer)], T[("down", layer)]
                for i in range(4):
                    for kg in range(6):
                        nk = min(4, HT - 4 * kg)
                        if i == 0:
                            pe.wait_ge(f_gl, HT * layer + 4 * kg + nk + 2)
                        product(u + 6 * i + kg, t + 2 * i, nk, 4 * kg, gh, gl, first=kg == 0, last=kg == 5)
                    if i:
                        add_square(r + 1, 2 * i - 2)
                        add_square(r + 1, 2 * i - 1)
                add_square(r + 1, KD - 2)
                add_square(r + 1, KD - 1)
                pe.wait_ge(p_lo, PK * (layer + 1))
                for i in range(2):
                    product(U[("proj", layer)] + i, T[("proj", layer)] + 4 * i, PK, 0, ph, pl, tiles=4)
                pe.wait_ge(ul_done, KD * SPLIT[r + 1] + KD)
                u, t = U[("gate", layer)], T[("gate", layer)]
                for i in range(4):
                    for kg in range(2):
                        product(u + 2 * i + kg, t + 2 * i, 4, 4 * kg, uh, ul, first=kg == 0, last=kg == 1)
                    if i:
                        add_square(r + 2, 2 * i - 2)
                        add_square(r + 2, 2 * i - 1)
                add_square(r + 2, KD - 2)
                add_square(r + 2, KD - 1)

            for b in range(SB):
                for half in range(2):
                    if b == 0:
                        pe.wait_ge(hn_done, 4 * half + 4)
                    pe.wait_ge(evac, T["final"] + 2 * b + half - 3)
                    for k in range(4):
                        mm_ = pe.transpose(bank(T["final"] + 2 * b + half)[:, k * P:(k + 1) * P],
                                           hn[:, 4 * half + k, b * P:(b + 1) * P], eye[:])
                    mm_.then_inc(filled, 1)


_INS = ['x', 'p', 'ssd_w_in', 'ssd_conv_w', 'ssd_conv_b', 'ssd_dt_bias', 'ssd_a_log', 'ssd_d', 'ssd_norm_w',
        'ssd_w_out', 's5_a_re', 's5_a_im', 's5_log_step', 's5_b_re', 's5_b_im', 's5_c_re', 's5_c_im', 's5_d',
        's5_w_glu', 's5_b_glu', 'mix_norm_w', 'ffn_norm_w', 'ffn_w_up', 'ffn_conv_w', 'ffn_conv_b', 'ffn_w_down',
        'ple_norm_w', 'ple_w_gate', 'ple_w_proj', 'final_norm_w']


def kernel(**inputs):
    import numpy as _np
    import concourse.bacc as _bacc
    from concourse import mybir as _mybir
    from concourse.bass_utils import run_bass_kernel_spmd as _run

    nc = _bacc.Bacc("TRN2", target_bir_lowering=False, num_devices=1)
    arrays, args = {}, {}
    for name in _INS:
        a = _np.ascontiguousarray(inputs[name])
        arrays[f"in_{name}"] = a
        args[name] = nc.dram_tensor(f"in_{name}", a.shape, _mybir.dt.from_np(a.dtype), kind="ExternalInput").ap()
    out = nc.dram_tensor("out_0", inputs["x"].shape, _mybir.dt.float32, kind="ExternalOutput").ap()
    bidir_hybrid_kernel(nc, args, out)
    r = _run(nc, [arrays], core_ids=[0])
    return r.results[0]["out_0"]
```

```python
import concourse.bass as bass
from concourse import mybir
from contextlib import ExitStack

F32 = mybir.dt.float32
F32R = mybir.dt.float32r
ACT = mybir.ActivationFunctionType
ALU = mybir.AluOpType

P = 128
EPS = 1e-6
PI = 3.14159265358979
PI_BELOW = 3.1415925
TWO_PI_HI = 6.28125
TWO_PI_MID = 0.0019350051879882812
TWO_PI_LO = 2.0 * 3.141592653589793 - TWO_PI_HI - TWO_PI_MID
ROUND_MAGIC = 12582912.0


class Plan:

    def __init__(self, groups, ffn_pairs):
        self.tile, self.fill, self.unit = {}, {}, {}
        tiles = fills = 0

        def tile(name, n, streamed=False):
            nonlocal tiles, fills
            self.tile[name] = tiles
            tiles += n
            if not streamed:
                self.fill[name] = fills
                fills += n

        tile("params", 2)
        tile("x", 8)
        tile("dt", 1, True)
        for g in range(groups):
            tile(("xbc", g), 6, True)
            tile(("z", g, 0), 2, True)
            tile(("xseq", g), 4)
            tile(("bseq", g), 1)
            tile(("cb", g), 1)
            tile(("z", g, 1), 2, True)
            if g == 0:
                tile("seq", 1)
                tile("sums", 1)
                tile("totals", 1)
            tile(("state", g, 0), 4)
            if g:
                tile(("out", g - 1, 0), 2, True)
            tile(("state", g, 4), 2)
            tile(("yoff", g), 6)
            if g:
                for i in range(1, 4):
                    tile(("out", g - 1, i), 2, True)
        for i in range(4):
            tile(("out", groups - 1, i), 2, True)
        for layer in range(2):
            if layer == 1:
                tile("s5", 64)
                tile("glu", 16, True)
            tile(("up", layer), 4 * ffn_pairs, True)
            tile(("p", layer), 2)
            tile(("down", layer), 8, True)
            tile(("proj", layer), 8, True)
            tile(("gate", layer, 0), 4, True)
            if layer == 0:
                tile("c5", 8)
            tile(("gate", layer, 1), 4, True)
        tile("final", 8)

        units = 0
        mixer = [("dt", 1)]
        for g in range(groups):
            mixer += [(("xbc", g), 6), (("z", g), 4)] + ([(("out", g - 1), 4)] if g else [])
        mixer += [(("out", groups - 1), 4)]
        for name, n in (mixer
                        + [(("up", 0), 4 * ffn_pairs), (("down", 0), 24), (("proj", 0), 2), (("gate", 0), 8)]
                        + [("glu", 16), (("up", 1), 4 * ffn_pairs), (("down", 1), 24), (("proj", 1), 2),
                           (("gate", 1), 8)]):
            self.unit[name] = units
            units += n
        self.units = units


def bidir_hybrid_kernel(nc, A, out):
    _, SEQ, D = A["x"].shape
    KD = D // P
    SB = SEQ // P
    INNER = A["ssd_norm_w"].shape[1]
    HEADS = A["ssd_d"].shape[1]
    HD = INNER // HEADS
    GROUPS = 4
    HPG = HEADS // GROUPS
    GC = INNER // GROUPS
    GT = GC // P
    CONV_T = A["ssd_conv_b"].shape[1] // P
    XBC0 = INNER
    HID = A["ffn_w_down"].shape[1]
    HT = HID // P
    PAIRS = HT // 2
    PLE = A["p"].shape[3]
    PK = PLE // P
    TAU = 4
    NCH = SEQ // TAU
    S5G = A["s5_b_re"].shape[1]
    S5P = A["s5_b_re"].shape[2]
    S5H = A["s5_b_re"].shape[3]
    J = S5G * S5P // P
    NB = D // P
    BP = J // NB
    CH = 2 * S5H

    plan = Plan(GROUPS, PAIRS)
    T, FILL, U, UNITS = plan.tile, plan.fill, plan.unit, plan.units

    C_MIX, C_FFN, C_PLE, C_FIN = 0, 16, 32, 48
    C_BGLU, C_S5D, C_SSDN, C_CONVB = 56, 72, 80, 96
    C_CONVW = P
    C_FCW = 2 * P
    C_FCB = C_FCW + 2 * 3 * 2 * HT
    C_A = 5 * P
    C_STEP = 6 * P

    with ExitStack() as ctx:
        def sb(name, shape, dt=F32, where=ctx):
            return where.enter_context(nc.sbuf_tensor(name, shape, dt))

        def sem(name):
            return ctx.enter_context(nc.semaphore(name))

        h = sb("h", [P, KD, SEQ])
        w_raw = sb("w_raw", [P, 2, 1024])
        w_hi = [sb(f"w_hi{i}", [P, 1024], F32R) for i in range(2)]
        w_lo = [sb(f"w_lo{i}", [P, 1024], F32R) for i in range(2)]
        par = sb("par", [P, 7 * P])
        ones = sb("ones", [P, P])
        eye = sb("eye", [P, P])
        le = sb("le", [P, P])
        ge = sb("ge", [P, P])
        lt = sb("lt", [P, P])
        gt = sb("gt", [P, P])
        rstd = sb("rstd", [P, SEQ])
        var = sb("var", [P, SEQ])
        sq = sb("sq", [P, 2, SEQ])
        cin = sb("cin", [P, 2, SEQ + 4])
        cc = sb("cc", [P, 4, SEQ])
        d_row = sb("d_row", [P, HEADS])
        d_col = sb("d_col", [P, HEADS // 2])
        hvec = sb("hvec", [2 * HEADS, 4])

        layer0 = ExitStack()
        uh0 = sb("uh0", [P, KD, SEQ], F32R, layer0)
        ul0 = sb("ul0", [P, KD, SEQ], F32R, layer0)
        start = ExitStack()
        x_in = sb("x_in", [P, SB, D], where=start)
        stage = sb("stage", [P, 7, P], where=start)
        step_in = sb("step_in", [2 * J, 2], where=start)
        start.close()
        ssd = ExitStack()
        xT = sb("xT", [P, GT, SEQ], where=ssd)
        bT = sb("bT", [P, SEQ], where=ssd)
        cT = sb("cT", [P, SEQ], where=ssd)
        xseq = sb("xseq", [P, SB, GC], where=ssd)
        bseq = sb("bseq", [P, SB, P], where=ssd)
        cbT = sb("cbT", [P, SEQ], where=ssd)
        zs = sb("zs", [P, GT, SEQ], where=ssd)
        xd = sb("xd", [P, 2, GC], where=ssd)
        car = sb("car", [P, 2, SB - 1, GC], where=ssd)
        yo = sb("yo", [P, SB, GC], where=ssd)
        ytmp = sb("ytmp", [P, GC], where=ssd)
        rr = sb("rr", [P, 2, 2, SB, P], where=ssd)
        wf = sb("wf", [P, 2, SB, P], where=ssd)
        wb = sb("wb", [P, 2, SB, P], where=ssd)
        mm = sb("mm", [P, 2, 2, SEQ], where=ssd)
        dt_seq = sb("dt_seq", [P, SB, 2 * HEADS], where=ssd)
        ad_seq = sb("ad_seq", [P, SB, 2 * HEADS], where=ssd)
        epq = sb("epq", [P, 2, SB, 2 * HEADS], where=ssd)
        etot = sb("etot", [P, SB, 2 * HEADS], where=ssd)
        yh = sb("yh", [P, GT, SEQ], F32R, ssd)
        yl = sb("yl", [P, GT, SEQ], F32R, ssd)
        dtT = mm[0:2 * HEADS, 0, 0, :]
        adT = mm[0:2 * HEADS, 0, 1, :]
        spz = mm[0:2 * HEADS, 1, 0, :]
        spw = mm[0:2 * HEADS, 1, 1, :]
        speq = wf[0:2 * HEADS, 0].rearrange("p c l -> p (c l)")
        ssd.close()

        def ffn_memory(layer, where):
            m = ExitStack()
            gh = sb(f"gh{layer}", [P, HT, SEQ], F32R, m)
            gl = sb(f"gl{layer}", [P, HT, SEQ], F32R, m)
            keep = sb(f"p_in{layer}", [P, SB, PLE], where=m)
            ph = sb(f"ph{layer}", [P, PK, SEQ], F32R, m)
            pl = sb(f"pl{layer}", [P, PK, SEQ], F32R, m)
            m.close()
            m = ExitStack()
            pp = sb(f"pproj{layer}", [P, KD, SEQ], where=m)
            m.close()
            return gh, gl, keep, ph, pl, pp

        ffn0 = ffn_memory(0, layer0)
        layer0.close()

        s5 = ExitStack()
        u5 = sb("u5", [P, KD, SEQ], where=s5)
        pw = sb("pw", [P, TAU + 1, 2, 4, BP, S5H], where=s5)
        m4 = sb("m4", [P, 2 * BP, NCH], where=s5)
        kT = sb("kT", [P, BP, P], where=s5)
        vblk = sb("vblk", [P, 2, 2, BP, TAU, CH], where=s5)
        vT = sb("vT", [P, 2, 2, BP, P], where=s5)
        cw = sb("cw", [P, 2, 2, J, S5H], where=s5)
        b5 = sb("b5", [P, 2, J, S5H], where=s5)
        zz = sb("zz", [P, 2, 2 * BP, NCH], where=s5)
        ta = sb("ta", [P, 2 * BP, NCH], where=s5)
        tb = sb("tb", [P, 2 * BP, NCH], where=s5)
        cblk_both = sb("cblk", [P, 2, 2, 2, BP, TAU + 1, CH], where=s5)
        cblk = [cblk_both[:, i] for i in range(2)]
        ulift = [sb(f"ulift{i}", [P, BP, NCH], where=s5) for i in range(2)]
        rot = sb("rot", [P, 2, 2 * BP, NCH], where=s5)
        xs = sb("xs", [P, 4, 2, BP, NCH + 1], where=s5)
        ddiag = sb("ddiag", [P, BP, P], where=s5)
        smask = sb("smask", [P, 2, NCH], where=s5)
        px = sb("px", [P, 2, 4 * BP, S5H], where=s5)
        py = sb("py", [P, 2, 4 * BP, S5H], where=s5)
        c_in = cblk_both[:].rearrange("p i a d j t h -> p (i a d j t h)")[:, 0:4 * NB * P].rearrange(
            "p (c b q) -> p c b q", c=4, b=NB)
        cst = zz[:].rearrange("p a x k -> p (a x k)").rearrange(
            "p (c b j q) -> p c b j q", c=4, b=NB, j=BP)
        s5.close()
        high = ExitStack()
        sb("below", [P, 2 * KD * SEQ + 2 * HT * SEQ + SB * PLE + 2 * PK * SEQ], where=high)
        v5 = sb("v5", [P, 13, 2 * J], where=high)
        lamx = sb("lamx", [P, 2, NB, 4 * BP], where=high)
        m4v = sb("m4v", [P, 2 * J], where=high)
        dlift = sb("dlift", [P, NB, BP], where=high)
        tn = sb("tn", [P, 2, 7, 2 * J], where=high)
        high.close()
        layer1 = ExitStack()
        uh1 = sb("uh1", [P, KD, SEQ], F32R, layer1)
        ul1 = sb("ul1", [P, KD, SEQ], F32R, layer1)
        glu = ExitStack()
        gh5 = sb("gh5", [P, KD, SEQ], F32R, glu)
        gl5 = sb("gl5", [P, KD, SEQ], F32R, glu)
        glu.close()
        ffn1 = ffn_memory(1, layer1)
        layer1.close()
        last = ExitStack()
        hn = sb("hn", [P, KD, SEQ], where=last)
        o_sb = sb("o_sb", [P, SB, D], where=last)
        last.close()
        UH, UL = [uh0, uh1], [ul0, ul1]
        FFN = [ffn0, ffn1]

        ring = ctx.enter_context(nc.psum_tensor("ring", [P, 4, SEQ], F32))
        pe_e = ctx.enter_context(nc.psum_tensor("pe_e", [P, 2, SEQ], F32))
        pe_y = ctx.enter_context(nc.psum_tensor("pe_y", [P, SEQ], F32))
        pe_s = ctx.enter_context(nc.psum_tensor("pe_s", [P, SEQ], F32))

        loaded = [sem("w_loaded0"), sem("w_loaded1")]
        hi_done, lo_done = sem("w_hi_done"), sem("w_lo_done")
        unit_done = sem("unit_done")
        filled, evac = sem("tile_filled"), sem("tile_evacuated")
        in_x, in_par, in_small = sem("x_loaded"), sem("params_loaded"), sem("small_loaded")
        masks = sem("masks_ready")
        stage_zero = sem("stage_zeroed")
        c5_half, cw_done = sem("c_upper_taken"), sem("cq_done")
        p_lo = sem("p_lo")
        step_x = sem("step_spread")
        sq_done, sq_used = sem("square_done"), sem("square_summed")
        var_done, std_done, rstd_done = sem("variance_done"), sem("std_done"), sem("rstd_done")
        h_upd = sem("h_updated")
        uh_done, ul_done = sem("u_hi_done"), sem("u_lo_done")
        dt_done = sem("dt_done")
        sp_step = sem("softplus_step")
        dtx, adt = sem("dt_softplus"), sem("dt_a_done")
        e_done = sem("decays_exp_done")
        eq_done = sem("decay_dt_done")
        tap0, taps, silu = sem("conv_tap0"), sem("conv_taps"), sem("conv_silu")
        z_silu = sem("z_silu")
        xd_done, car_mul = sem("x_decayed"), sem("carry_decayed")
        yo_add = sem("yoff_added")
        r_done, e_full, exp_done = sem("masked_logs"), sem("exponents_filled"), sem("decay_exp")
        w_done, m_done, m_half = sem("dt_weights"), sem("m_done"), sem("m_half")
        y_full, y_skip, gated = sem("y_filled"), sem("y_skip_added"), sem("y_gated")
        gsq, gsq_used = sem("group_square"), sem("group_summed")
        gvar, gstd, grstd = sem("group_variance"), sem("group_std"), sem("group_rstd")
        yn_done, yh_done, yl_done = sem("y_normed"), sem("y_hi"), sem("y_lo")
        f_c0, f_taps, f_silu = sem("ffn_tap0"), sem("ffn_taps"), sem("ffn_silu")
        f_gv, f_gh, f_gl = sem("ffn_product"), sem("ffn_product_hi"), sem("ffn_product_lo")
        p_loaded = [sem("p0_loaded"), sem("p1_loaded")]
        p_hi = sem("p_hi")
        g_sig, g_mul = sem("gate_sigmoid"), sem("gate_product")
        u5_done = sem("s5_input")
        v_act, v_dve = sem("s5_vec_act"), sem("s5_vec_dve")
        c_loaded, b_loaded = sem("c_loaded"), sem("b_loaded")
        s5_zero = sem("s5_zeroed")
        pw0 = sem("power0_ready")
        pw_x, pw_r = sem("power_products"), sem("power_ready")
        blk = sem("block_diagonals")
        rot_x, rot_r = sem("rotation_products"), sem("rotation_ready")
        lift = sem("u_lifted")
        k_full, k_evac = sem("kernel_filled"), sem("kernel_evacuated")
        spin = sem("rotated")
        scan = sem("scanned")
        xs_r = sem("states_ready")
        y5_full, y5_gelu = sem("s5_y_filled"), sem("s5_gelu")
        d_lift, d_diag = sem("s5_d_lifted"), sem("s5_d_diagonal")
        m4_r = sem("decay_row_ready")
        g5_hi, g5_lo = sem("g_hi"), sem("g_lo")
        glu_sig, glu_mul = sem("glu_sigmoid"), sem("glu_product")
        hn_done = sem("h_normed")
        stored = sem("output_stored")

        def bank(t):
            return ring[:, t % 4, :]

        def col(c):
            return par[:, c:c + 1]

        def dcol(c):
            return par[:, bass.ds(c, 1)]

        def h_ready(r, m):
            if r == 0:
                return evac, T["x"] + m + 1
            if r == 1:
                return evac, T[("out", GROUPS - 1, 0)] + m + 1
            if r in (2, 5):
                return evac, T[("down", r // 3)] + m + 1
            return h_upd, {3: 0, 4: KD, 6: 2 * KD}[r] + m + 1

        SPLIT = {0: 0, 1: 1, 2: 2, 4: 3, 5: 4}
        NORM_COL = {0: C_MIX, 1: C_FFN, 2: C_PLE, 3: C_MIX + KD, 4: C_FFN + KD, 5: C_PLE + KD, 6: C_FIN}

        def unit_size(u):
            for name in ("dt",):
                if u == U[name]:
                    return KD * 2 * HEADS
            for layer in range(2):
                k = u - U[("down", layer)]
                if 0 <= k < 24 and k % 6 == 5:
                    return 512
            return 1024

        def loads_by(u):
            two = [U[("xbc", g)] + 4 + kg for g in range(GROUPS) for kg in range(2)]
            return 16 * (u // 2 + 1) + 16 * sum(1 for t in two if t <= u and t % 2 == u % 2)

        def part(buf, u, k):
            n = unit_size(u)
            b = buf[:, u % 2, 0:n] if buf is w_raw else buf[u % 2][:, 0:n]
            return b.rearrange("p (k n) -> p k n", k=k)

        block = ctx.enter_context(nc.Block())

        @block.sync
        def _(sp):
            def load(u, src, at=0, k=4):
                if u >= 2:
                    sp.wait_ge(lo_done, at + (u - 1))
                sp.dma_start(part(w_raw, u, k), src).then_inc(loaded[u % 2], 16)

            def rows(w, k0, nk, c0, nc_):
                return w[k0 * P:(k0 + nk) * P, c0:c0 + nc_].rearrange("(k p) n -> p k n", p=P)

            sp.dma_start(x_in[:], A["x"][0].rearrange("(b p) d -> p b d", p=P)).then_inc(in_x, 16)

            sp.wait_ge(stage_zero, 1)

            def vec(group, r0, ap):
                sp.dma_start(stage[r0:r0 + ap.shape[0], group, :], ap).then_inc(in_par, 16)

            vec(0, C_MIX, A["mix_norm_w"].rearrange("l (c p) -> (l c) p", p=P))
            vec(0, C_FFN, A["ffn_norm_w"].rearrange("l (c p) -> (l c) p", p=P))
            vec(0, C_PLE, A["ple_norm_w"].rearrange("l (c p) -> (l c) p", p=P))
            vec(0, C_FIN, A["final_norm_w"].rearrange("(c p) -> c p", p=P))
            vec(0, C_BGLU, A["s5_b_glu"].rearrange("l (c p) -> (l c) p", p=P))
            vec(0, C_S5D, A["s5_d"].rearrange("l (c p) -> (l c) p", p=P))
            vec(0, C_SSDN, A["ssd_norm_w"].rearrange("l (c p) -> (l c) p", p=P))
            vec(0, C_CONVB, A["ssd_conv_b"].rearrange("l (c p) -> (l c) p", p=P))
            vec(1, 0, A["ssd_conv_w"].rearrange("l t (c p) -> (l t c) p", p=P))
            fcw = A["ffn_conv_w"].rearrange("l t (c p) -> (l t c) p", p=P)
            vec(2, 0, fcw[0:P])
            vec(3, 0, fcw[P:2 * P])
            vec(4, 0, fcw[2 * P:])
            vec(4, C_FCB - 4 * P, A["ffn_conv_b"].rearrange("l (c p) -> (l c) p", p=P))
            vec(5, 0, A["s5_a_re"].rearrange("l d (j g) p -> (l d j) (g p)", g=2))
            vec(5, 2 * J, A["s5_a_im"].rearrange("l d (j g) p -> (l d j) (g p)", g=2))
            sp.dma_start(step_in[:], A["s5_log_step"].rearrange("l d (j g) -> (l d j) g", g=2)).then_inc(in_par, 16)
            sp.dma_start(hvec[:, 0:1], A["ssd_dt_bias"].rearrange("l d (h a) -> (l d h) a", a=1)).then_inc(in_small, 16)
            sp.dma_start(hvec[:, 1:2], A["ssd_a_log"].rearrange("l d (h a) -> (l d h) a", a=1)).then_inc(in_small, 16)
            sp.dma_start(d_row[:], A["ssd_d"][0].partition_broadcast(P)).then_inc(in_small, 16)
            load(U["dt"], rows(A["ssd_w_in"][0], 0, KD, XBC0 + CONV_T * P, 2 * HEADS), k=KD)

            w_in = A["ssd_w_in"][0]
            bc = w_in[:, XBC0 + INNER:XBC0 + INNER + 2 * GROUPS * P].rearrange(
                "(k p) (two n) -> p k two n", p=P, two=2)

            def ssd_loads(g):
                u = U[("xbc", g)]
                for i in range(2):
                    for kg in range(2):
                        load(u + 2 * i + kg, rows(w_in, 4 * kg, 4, XBC0 + g * GC + 256 * i, 256))
                for kg in range(2):
                    if u + 4 + kg >= 2:
                        sp.wait_ge(lo_done, u + 4 + kg - 1)
                    dst = w_raw[:, (u + 4 + kg) % 2, :].rearrange("p (k two n) -> p k two n", k=4, two=2)
                    for two in range(2):
                        sp.dma_start(dst[:, :, two, :], bc[:, 4 * kg:4 * kg + 4, two, g * P:(g + 1) * P]
                                     ).then_inc(loaded[(u + 4 + kg) % 2], 16)
                for i in range(2):
                    for kg in range(2):
                        load(U[("z", g)] + 2 * i + kg, rows(w_in, 4 * kg, 4, g * GC + 256 * i, 256))

            def out_loads(g):
                for i in range(4):
                    load(U[("out", g)] + i, rows(A["ssd_w_out"][0], GT * g, GT, 256 * i, 256))

            for g in range(GROUPS):
                ssd_loads(g)
                if g:
                    out_loads(g - 1)
            out_loads(GROUPS - 1)

            for layer in range(2):
                if layer == 1:
                    u = U["glu"]
                    w = A["s5_w_glu"][0]
                    for i in range(4):
                        for half in range(2):
                            for kg in range(2):
                                load(u + 4 * i + 2 * half + kg, rows(w, 4 * kg, 4, half * D + 256 * i, 256))
                u = U[("up", layer)]
                wk = A["ffn_w_up"][layer].rearrange("(k p) n -> p k n", p=P)
                with sp.Fori(0, PAIRS) as i:
                    for half in range(2):
                        for kg in range(2):
                            load(u + 2 * half + kg, wk[:, 4 * kg:4 * kg + 4, bass.ds(i * 256 + half * HID, 256)],
                                 at=i * 4)
                sp.wait_ge(ul_done, (2, 4)[layer] * KD)
                sp.dma_start(FFN[layer][2][:], A["p"][layer, 0].rearrange("(b q) n -> q b n", q=P)
                             ).then_inc(p_loaded[layer], 16)
                u = U[("down", layer)]
                for i in range(4):
                    for kg in range(6):
                        nk = min(4, HT - 4 * kg)
                        load(u + 6 * i + kg, rows(A["ffn_w_down"][layer], 4 * kg, nk, 256 * i, 256), k=nk)
                for i in range(2):
                    load(U[("proj", layer)] + i, rows(A["ple_w_proj"][layer], 0, PK, 512 * i, 512), k=PK)
                for i in range(4):
                    for kg in range(2):
                        load(U[("gate", layer)] + 2 * i + kg, rows(A["ple_w_gate"][layer], 4 * kg, 4, 256 * i, 256))
                        if layer == 0 and (i, kg) == (1, 0):
                            sp.wait_ge(evac, T[("down", 0)] + 8)
                            for a, name in enumerate(("s5_c_re", "s5_c_im")):
                                for d in range(2):
                                    for half in range(2):
                                        sp.dma_start(c_in[:, 2 * a + d, :, 64 * half:64 * half + 64],
                                                     A[name][0, d].rearrange("(b g) h p -> (g h) b p", b=NB)
                                                     ).then_inc(c_loaded, 16)
                            for a, name in enumerate(("s5_b_re", "s5_b_im")):
                                sp.dma_start(b5[:, a, :, :], A[name][0].rearrange("(j g) p h -> (g p) j h", g=2)
                                             ).then_inc(b_loaded, 16)

            o_v = out[0].rearrange("(b p) d -> p b d", p=P)
            for b in range(SB):
                sp.wait_ge(evac, T["final"] + 2 * b + 2)
                sp.dma_start(o_v[:, b, :], o_sb[:, b, :]).then_inc(stored, 16)
            sp.wait_ge(stored, 16 * SB)

        @block.gpsimd
        def _(pool):
            pool.memset(ones[:], 1.0).then_inc(masks, 1)
            for m in (le, ge, lt, gt):
                pool.memset(m[:], 1.0).then_inc(masks, 1)
            pool.memset(eye[:], 0.0).then_inc(masks, 1)
            pool.wait_ge(masks, 6)
            for m, sign, base in ((le, 1, 0), (ge, -1, 0), (lt, 1, -1), (gt, -1, -1)):
                pool.affine_select(out=m[:], in_=m[:], compare_op=ALU.is_ge, fill=0.0, base=base,
                                   pattern=[[sign, P]], channel_multiplier=-sign).then_inc(masks, 1)
            pool.affine_select(out=eye[:], in_=eye[:], compare_op=ALU.not_equal, fill=1.0, base=0,
                               pattern=[[-1, P]], channel_multiplier=1).then_inc(masks, 1)

            pool.wait_ge(evac, T["c5"] + 8)
            for i in range(2):
                pool.memset(cblk[i], 0.0).then_inc(s5_zero, 1)
            pool.memset(xs[:], 0.0).then_inc(s5_zero, 1)
            pool.memset(smask[:], 1.0).then_inc(s5_zero, 1)
            pool.wait_ge(s5_zero, 4)
            pool.memset(smask[:, 0, 0:1], 0.0).then_inc(s5_zero, 1)
            pool.memset(smask[:, 1, NCH - 1:NCH], 0.0).then_inc(s5_zero, 1)
            pool.wait_ge(h_upd, KD)
            pool.memset(vblk[:], 0.0).then_inc(s5_zero, 1)
            pool.wait_ge(s5_zero, 7)
            with pool.Fori(0, NB // 2) as i:
                for slot in range(2):
                    b = i * 2 + slot
                    pool.wait_ge(u5_done, b + 1)
                    pool.wait_ge(y5_full, b + 1)
                    for j in range(BP):
                        for s in range(TAU):
                            if slot or j or s:
                                pool.wait_ge(lift, b * 16 + (TAU * j + s))
                            pool.tensor_copy(ulift[slot][CH * s:CH * s + CH, j, :],
                                             u5[CH * j:CH * j + CH, bass.ds(b, 1), s::TAU].rearrange(
                                                 "p b k -> p (b k)")).then_inc(lift, 1)

        @block.scalar
        def _(act):
            def hi(u, at=0, mul=0):
                if u >= UNITS:
                    return
                act.wait_ge(loaded[u % 2], loads_by(u) + at * 8)
                if u >= 2:
                    act.wait_ge(unit_done, at + (u - 1))
                n = unit_size(u)
                act.activation(w_hi[u % 2][:, 0:n], w_raw[:, u % 2, 0:n], ACT.Copy).then_inc(hi_done, 1)

            rounded = [-1]

            def hi_to(u):
                while rounded[0] < u:
                    rounded[0] += 1
                    hi(rounded[0])

            def squares(r, m):
                act.wait_ge(*h_ready(r, m))
                if 8 * r + m >= 2:
                    act.wait_ge(sq_used, KD * r + m - 1)
                act.activation(sq[:, m % 2, :], h[:, m, :], ACT.Square).then_inc(sq_done, 1)

            def u_hi(r, m, uh):
                act.wait_ge(*h_ready(r, m))
                act.activation(uh[:, m, :], h[:, m, :], ACT.Identity, scale=col(NORM_COL[r] + m)).then_inc(uh_done, 1)

            def std(r):
                act.wait_ge(var_done, r + 1)
                act.activation(var[:], var[:], ACT.Sqrt).then_inc(std_done, 1)

            hi_to(0)
            act.wait_ge(evac, 2)
            for m in range(KD):
                squares(0, m)
                u_hi(0, m, uh0)
            std(0)
            def dt_steps():
                act.wait_ge(in_small, 48)
                act.activation(hvec[:, 2:3], hvec[:, 1:2], ACT.Exp).then_inc(dtx, 1)
                act.wait_ge(evac, T["dt"] + 1)
                act.activation(dtT, dtT, ACT.Identity, bias=hvec[:, 0:1]).then_inc(dtx, 1)
                act.wait_ge(dtx, 2)
                act.activation(spz, dtT, ACT.Abs).then_inc(dtx, 1)
                act.wait_ge(dtx, 3)
                act.activation(spz, spz, ACT.Exp, scale=-1.0).then_inc(dtx, 1)
                act.wait_ge(sp_step, 1)
                act.activation(adT, spw, ACT.Ln).then_inc(dtx, 1)

            def dt_sums():
                act.wait_ge(evac, T["sums"] + 1)
                act.activation(epq[:], epq[:], ACT.Exp).then_inc(e_done, 1)
                act.wait_ge(evac, T["totals"] + 1)
                act.activation(etot[:], etot[:], ACT.Exp).then_inc(e_done, 1)

            def masked_logs(n):
                if n >= 1:
                    act.wait_ge(e_full, n)
                for d, m in ((0, le), (1, ge)):
                    for k in range(2):
                        for c in range(SB):
                            at = HEADS * d + 2 * n + k
                            act.activation(rr[:, d, k, c, :], m[:], ACT.Copy, scale=ad_seq[:, c, at:at + 1]
                                           ).then_inc(r_done, 1)

            hi_to(1)
            for g in range(GROUPS):
                u, z = U[("xbc", g)], U[("z", g)]
                w = z + 4
                for i in range(3):
                    hi_to(u + 2 * i + 3)
                    chans = [g * GT + 2 * i, g * GT + 2 * i + 1] if i < 2 else [INNER // P + g, INNER // P + GROUPS + g]
                    for j in range(2):
                        q = 6 * g + 2 * i + j
                        act.wait_ge(evac, T[("xbc", g)] + 2 * i + j + 1)
                        if q >= 4:
                            act.wait_ge(silu, q - 3)
                        act.activation(cc[:, q % 4, :], cin[:, q % 2, 0:SEQ], ACT.Identity,
                                       scale=col(C_CONVW + chans[j]), bias=col(C_CONVB + chans[j])).then_inc(tap0, 1)
                    hi_to(u + 2 * i + 4)
                    if g >= 1 and i == 0:
                        act.wait_ge(yl_done, GT * g)
                    for j in range(2):
                        q = 6 * g + 2 * i + j
                        dst = xT[:, 2 * i + j, :] if i < 2 else (bT, cT)[j][:]
                        act.wait_ge(taps, 8 * (3 * g + i) + 6 + j + 1)
                        act.activation(dst, cc[:, q % 4, :], ACT.Silu).then_inc(silu, 1)
                hi_to(z + 3)
                for i in range(2):
                    if i == 1:
                        if g:
                            masked_logs(GT * g)
                        else:
                            dt_steps()
                        hi_to(z + 5)
                    for j in range(2):
                        act.wait_ge(evac, T[("z", g, i)] + j + 1)
                        act.activation(zs[:, 2 * i + j, :], zs[:, 2 * i + j, :], ACT.Silu).then_inc(z_silu, 1)
                if g == 0:
                    dt_sums()
                    act.wait_ge(adt, 2)
                    act.wait_ge(evac, T["seq"] + 1)
                    masked_logs(0)

                def decays(hp):
                    n = GT * g + hp
                    act.wait_ge(e_full, n + 1)
                    if n >= 2:
                        act.wait_ge(y_full, n - 1)
                    act.activation(mm[:, n % 2, :, :], pe_e[:], ACT.Exp).then_inc(exp_done, 1)
                    if hp + 1 < GT:
                        masked_logs(n + 1)

                decays(0)
                if g:
                    hi_to(w + 2)
                decays(1)
                for hp in range(GT + 1):
                    if hp + 2 < GT:
                        decays(hp + 2)
                    if hp + 1 < GT and g:
                        hi_to(w + hp + 3)
                    if hp >= 1:
                        n = GT * g + hp - 1
                        act.wait_ge(gated, n + 1)
                        if n >= 2:
                            act.wait_ge(gsq_used, n - 1)
                        act.activation(sq[:, n % 2, :], xT[:, hp - 1, :], ACT.Square).then_inc(gsq, 1)
                act.wait_ge(gvar, g + 1)
                act.activation(var[:], var[:], ACT.Sqrt).then_inc(gstd, 1)
                if g < GROUPS - 1:
                    hi_to(U[("xbc", g + 1)] + 2)
                if g:
                    act.wait_ge(unit_done, w + 4)
                for m in range(GT):
                    act.wait_ge(yn_done, GT * g + m + 1)
                    act.activation(yh[:, m, :], zs[:, m, :], ACT.Copy).then_inc(yh_done, 1)
            for i in range(4):
                hi_to(U[("out", GROUPS - 1)] + i + 2)
                for m in (2 * i, 2 * i + 1):
                    squares(1, m)
                    u_hi(1, m, uh0)

            def vec(dst, src, f, need, scale=1.0):
                if need:
                    act.wait_ge(v_dve, need)
                act.activation(v5[:, dst, :], src, f, scale=scale).then_inc(v_act, 1)

            for layer in range(2):
                gh, gl, p_in, ph, pl, pproj = FFN[layer]
                if layer == 1:
                    act.sem_inc(blk, 1)
                    act.sem_inc(y5_gelu, 1)
                    act.sem_inc(k_evac, 1)
                    act.wait_ge(b_loaded, 32)
                    act.wait_ge(cw_done, 1)
                    act.wait_ge(d_lift, 16)
                    act.wait_ge(h_upd, KD)

                    def power0(b):
                        act.wait_ge(blk, b * 16 + 1)
                        for a in range(2):
                            for d in range(2):
                                act.activation(pw[:, 0, a, d, :, :], cw[:, a, d, bass.ds(b * BP, BP), :],
                                               ACT.Copy).then_inc(pw0, 1)
                                act.activation(pw[:, 0, a, 2 + d, :, :], b5[:, a, bass.ds(b * BP, BP), :],
                                               ACT.Copy).then_inc(pw0, 1)

                    def diagonals(b, slot, first=False):
                        act.wait_ge(pw_r, b * (2 * TAU) + 2 * TAU)
                        act.wait_ge(y5_full, b + 1)
                        if not first:
                            act.wait_ge(k_full, b)
                        if first:
                            act.wait_ge(s5_zero, 7)
                        for half in range(2):
                            rows = slice(64 * half, 64 * half + 64)
                            chs = slice(S5H * half, S5H * half + S5H)
                            for a in range(2):
                                for d in range(2):
                                    dst = vblk[rows, a, d, :, ::(-1, 1)[d], chs]
                                    act.activation(dst.rearrange("p j t h -> p t j h"), pw[rows, 0:TAU, a, 2 + d, :, :],
                                                   ACT.Copy).then_inc(blk, 1)
                                    dst = cblk[slot][rows, a, d, :, ::(1, -1)[d], chs]
                                    act.activation(dst.rearrange("p j t h -> p t j h"), pw[rows, :, a, d, :, :],
                                                   ACT.Copy, scale=(1.0, -1.0)[a]).then_inc(blk, 1)
                        for j in range(BP):
                            act.activation(ddiag[:, j, :], eye[:], ACT.Copy,
                                           scale=dlift[:, bass.ds(b, 1), j]).then_inc(d_diag, 1)

                    def tables(b, first=False):
                        for n in range(4):
                            act.wait_ge(filled, b * 8 + (FILL["s5"] + n + 1))
                            act.activation(vT[:, n // 2, n % 2].rearrange("p j q -> p (j q)"), bank(T["s5"] + n),
                                           ACT.Copy).then_inc(evac, 1)
                        if not first:
                            act.wait_ge(scan, b * 4)
                        for k in range(2 * BP):
                            act.activation(m4[:, k, :], smask[:, k // BP, :], ACT.Copy,
                                           scale=m4v[:, bass.ds(b * 8 + k, 1)]).then_inc(m4_r, 1)

                    def kernel_out(b):
                        act.wait_ge(k_full, b + 1)
                        act.wait_ge(y5_full, b + 2)
                        act.activation(kT[:].rearrange("p j q -> p (j q)"), pe_e[:, 0, :], ACT.Copy).then_inc(k_evac, 1)

                    def gelu(b):
                        act.wait_ge(y5_full, b + 3)
                        for j in range(BP):
                            for s in range(TAU):
                                act.activation(u5[CH * j:CH * j + CH, bass.ds(b, 1), s::TAU].rearrange(
                                    "p b k -> p (b k)"), pe_y[CH * s:CH * s + CH, j * NCH:(j + 1) * NCH],
                                    ACT.Gelu_apprx_tanh).then_inc(y5_gelu, 1)

                    def block_step(b, slot):
                        diagonals(b + 1, 1 - slot)
                        power0(b + 2)
                        tables(b + 1)
                        kernel_out(b + 1)
                        gelu(b)

                    power0(0)
                    std(3)
                    diagonals(0, 0, first=True)
                    power0(1)
                    tables(0, first=True)
                    kernel_out(0)
                    with act.Fori(0, NB // 2 - 1) as i:
                        for slot in range(2):
                            block_step(i * 2 + slot, slot)
                    diagonals(NB - 1, 1)
                    tables(NB - 1)
                    kernel_out(NB - 1)
                    act.wait_ge(filled, FILL["s5"] + 8 * NB)
                    act.wait_ge(y5_gelu, 16 * (NB - 2) + 1)
                    for m in range(NB - 2):
                        act.activation(gh5[:, m, :], u5[:, m, :], ACT.Copy).then_inc(g5_hi, 1)
                    gelu(NB - 2)
                    gelu(NB - 1)
                    act.wait_ge(y5_gelu, 16 * NB + 1)
                    for m in range(NB - 2, NB):
                        act.activation(gh5[:, m, :], u5[:, m, :], ACT.Copy).then_inc(g5_hi, 1)
                    u = U["glu"]
                    for i in range(4):
                        for half in range(2):
                            hi_to(u + 4 * i + 2 * half + 3)
                            if half:
                                for j in range(2):
                                    act.wait_ge(evac, T["glu"] + 4 * i + 2 + j + 1)
                                    act.activation(cc[:, 2 + j, :], cc[:, 2 + j, :], ACT.Sigmoid).then_inc(glu_sig, 1)
                        if i == 0:
                            act.wait_ge(g5_lo, KD)
                        for m in (2 * i, 2 * i + 1):
                            squares(4, m)
                            u_hi(4, m, uh1)
                std(1 + 3 * layer)
                u, t = U[("up", layer)], T[("up", layer)]
                hi_to(u + 2)
                done = layer * HT
                with act.Fori(0, PAIRS) as i:
                    for half in range(2):
                        hi(u + 2 * half + 3, at=i * 4)
                        for j in range(2):
                            act.wait_ge(evac, i * 4 + (t + 2 * half + j + 1))
                            act.wait_ge((f_gv, f_gl)[half], i * 2 + (done + j + 1))
                            c = 2 * 3 * HT * layer + half * HT + j
                            act.activation(cc[:, 2 * half + j, :], cin[:, j, 1:1 + SEQ], ACT.Identity,
                                           scale=dcol(i * 2 + (C_FCW + c)),
                                           bias=dcol(i * 2 + (C_FCB + 2 * HT * layer + half * HT + j))
                                           ).then_inc(f_c0, 1)
                        hi(u + 2 * half + 4, at=i * 4)
                        for j in range(2):
                            if half == 0:
                                act.wait_ge(f_taps, i * 8 + (4 * done + 2 + j + 2))
                                act.activation(cc[:, j, :], cc[:, j, :], ACT.Silu).then_inc(f_silu, 1)
                            else:
                                act.wait_ge(f_gv, i * 2 + (done + j + 3))
                                act.activation(gh[:, bass.ds(i * 2 + j, 1), :].rearrange("p a t -> p (a t)"),
                                               cc[:, 2 + j, :], ACT.Copy).then_inc(f_gh, 1)
                rounded[0] = U[("down", layer)] + 2
                for k in range(PK):
                    act.wait_ge(evac, T[("p", layer)] + k + 1)
                    act.activation(ph[:, k, :], cc[:, k, :], ACT.Copy).then_inc(p_hi, 1)
                u = U[("down", layer)]
                r = 2 + 3 * layer
                for i in range(4):
                    hi_to(u + 6 * i + 7)
                    for m in (2 * i, 2 * i + 1):
                        squares(r, m)
                        u_hi(r, m, UH[layer])
                    if (layer, i) == (0, 0):
                        vec(0, par[:, C_STEP:C_STEP + 2 * J], ACT.Exp, 0)
                        vec(1, v5[:, 1, :], ACT.Exp, 1)
                        vec(2, v5[:, 5, :], ACT.Sin, 8)
                        vec(3, v5[:, 5, :], ACT.Sin, 8, 0.5)
                    if (layer, i) == (0, 1):
                        for j in range(BP):
                            for s in range(TAU):
                                act.activation(dlift[CH * s:CH * s + CH, :, j], par[CH * j:CH * j + CH,
                                               C_S5D:C_S5D + NB], ACT.Copy).then_inc(d_lift, 1)
                hi_to(U[("proj", layer)] + 2)
                std(r)
                hi_to(U[("proj", layer)] + 3)
                u = U[("gate", layer)]
                for i in range(4):
                    hi_to(u + 2 * i + 3)
                    for m in (2 * i, 2 * i + 1):
                        act.wait_ge(evac, T[("gate", layer, m // 4)] + m % 4 + 1)
                        act.activation(cc[:, m % 4, :], cc[:, m % 4, :], ACT.Sigmoid).then_inc(g_sig, 1)
                    hi_to(min(u + 2 * i + 4, u + 9))
                    for m in (2 * i, 2 * i + 1):
                        squares(r + 1, m)
                if layer == 1:
                    std(r + 1)

        @block.vector
        def _(dve):
            def lo(u, at=0):
                if u >= UNITS:
                    return
                dve.wait_ge(hi_done, at + (u + 1))
                n = unit_size(u)
                dve.tensor_tensor(w_lo[u % 2][:, 0:n], w_raw[:, u % 2, 0:n], w_hi[u % 2][:, 0:n].bitcast(F32),
                                  ALU.subtract).then_inc(lo_done, 1)

            split = [-1]

            def lo_to(u):
                while split[0] < u:
                    split[0] += 1
                    lo(split[0])

            def u_lo(r, m, uh, ul):
                dve.wait_ge(uh_done, KD * SPLIT[r] + m + 1)
                dve.wait_ge(*h_ready(r, m))
                dve.scalar_tensor_tensor(out=ul[:, m, :], in0=h[:, m, :], scalar=col(NORM_COL[r] + m),
                                         in1=uh[:, m, :].bitcast(F32), op0=ALU.mult, op1=ALU.subtract
                                         ).then_inc(ul_done, 1)

            def rstd_of(r):
                dve.wait_ge(sq_used, KD * r + KD)
                dve.tensor_scalar(var[:], pe_s[:], 1.0 / D, EPS, ALU.mult, ALU.add).then_inc(var_done, 1)
                dve.wait_ge(std_done, r + 1)
                dve.reciprocal(rstd[:], var[:]).then_inc(rstd_done, 1)
                dve.wait_ge(rstd_done, r + 1)

            def take(name, k, dst):
                dve.wait_ge(filled, FILL[name] + k + 1)
                dve.tensor_copy(dst, bank(T[name] + k)[:, 0:dst.shape[1] if len(dst.shape) == 2 else SEQ]
                                ).then_inc(evac, 1)

            dve.memset(stage[:], 0.0).then_inc(stage_zero, 1)
            dve.memset(cin[:], 0.0).then_inc(f_taps, 1)
            dve.memset(cc[:, 0:2, 0:1], 0.0).then_inc(f_gv, 2)
            dve.memset(cc[:, 2:4, 0:1], 0.0).then_inc(f_gl, 2)
            dve.wait_ge(in_par, 16 * 16)
            dve.tensor_copy(stage[0:2 * J, 6, :].rearrange("p (g q) -> p g q", g=2),
                            step_in[:].unsqueeze(2).to_broadcast([2 * J, 2, S5P])).then_inc(step_x, 1)
            take("params", 0, par[:, 0:4 * P])
            dve.wait_ge(filled, FILL["params"] + 2)
            dve.tensor_copy(par[:, 4 * P:7 * P], bank(T["params"] + 1)[:, 0:3 * P]).then_inc(evac, 1)
            dve.wait_ge(evac, 2)
            for m in range(KD):
                take("x", m, h[:, m, :])
                u_lo(0, m, uh0, ul0)
            rstd_of(0)
            lo_to(0)
            dve.wait_ge(unit_done, 1)
            dve.tensor_tensor(dtT, bank(T["dt"])[0:2 * HEADS, :], rstd[0:2 * HEADS, :], ALU.mult).then_inc(evac, 1)
            lo_to(1)

            def dt_steps():
                count = [0]

                def sp_(op, *a, **k):
                    if count[0]:
                        dve.wait_ge(sp_step, count[0])
                    op(*a, **k).then_inc(sp_step, 1)
                    count[0] += 1

                dve.wait_ge(dtx, 4)
                sp_(dve.tensor_scalar, spw, spz, 1.0, None, ALU.add)
                dve.wait_ge(dtx, 5)
                sp_(dve.tensor_scalar, spw, spw, -1.0, None, ALU.add)
                sp_(dve.tensor_scalar, speq, spw, 0.0, None, ALU.is_equal)
                sp_(dve.tensor_tensor, adT, adT, speq, ALU.add)
                sp_(dve.tensor_tensor, spw, spw, speq, ALU.add)
                sp_(dve.reciprocal, spw, spw)
                sp_(dve.tensor_tensor, adT, adT, spw, ALU.mult)
                sp_(dve.tensor_tensor, adT, adT, spz, ALU.mult)
                sp_(dve.scalar_tensor_tensor, out=dtT, in0=dtT, scalar=0.0, in1=adT, op0=ALU.max, op1=ALU.add)
                dve.wait_ge(sp_step, count[0])
                dve.tensor_scalar(adT, dtT, hvec[:, 2:3], -1.0, ALU.mult, ALU.mult).then_inc(adt, 1)

            def dt_sums():
                dve.wait_ge(filled, FILL["seq"] + 1)
                s_t = bank(T["seq"]).rearrange("p (a c h) -> p a c h", a=2, c=SB)
                dve.tensor_copy(dt_seq[:], s_t[:, 0]).then_inc(adt, 1)
                dve.tensor_copy(ad_seq[:], s_t[:, 1]).then_inc(evac, 1)
                dve.wait_ge(filled, FILL["sums"] + 1)
                dve.tensor_copy(epq[:], bank(T["sums"]).rearrange("p (a c h) -> p a c h", a=2, c=SB)).then_inc(evac, 1)
                dve.wait_ge(filled, FILL["totals"] + 1)
                dve.tensor_copy(etot[:], bank(T["totals"])[:, 0:SB * 2 * HEADS].rearrange("p (c h) -> p c h", c=SB)
                                ).then_inc(evac, 1)
                dve.wait_ge(e_done, 2)
                dve.wait_ge(adt, 2)
                dve.tensor_tensor(epq[:, 1], epq[:, 1], dt_seq[:], ALU.mult).then_inc(eq_done, 1)
                dr = d_row[:].rearrange("p (t k) -> p t k", k=2)
                for k in range(2):
                    dve.tensor_copy(d_col[64 * k:64 * k + 64, :], dr[64 * k:64 * k + 64, :, k]).then_inc(eq_done, 1)
                dve.wait_ge(eq_done, 3)

            for g in range(GROUPS):
                u, z = U[("xbc", g)], U[("z", g)]
                w = z + 4
                for i in range(3):
                    lo_to(u + 2 * i + 2)
                    pr = 3 * g + i
                    chans = [g * GT + 2 * i, g * GT + 2 * i + 1] if i < 2 else [INNER // P + g, INNER // P + GROUPS + g]
                    dve.wait_ge(unit_done, u + 2 * i + 2)
                    if pr >= 1:
                        dve.wait_ge(taps, 8 * pr)
                    for j in range(2):
                        dve.tensor_tensor(cin[:, j, 2:2 + SEQ], bank(T[("xbc", g)] + 2 * i + j), rstd[:], ALU.mult
                                          ).then_inc(evac, 1)
                    lo_to(u + 2 * i + 3)
                    for tap in range(1, 5):
                        for j in range(2):
                            q = 6 * g + 2 * i + j
                            if tap == 1:
                                dve.wait_ge(tap0, q + 1)
                            else:
                                dve.wait_ge(taps, 8 * pr + 2 * (tap - 1) + j - 1)
                            dve.scalar_tensor_tensor(
                                out=cc[:, q % 4, :], in0=cin[:, j, tap:tap + SEQ],
                                scalar=col(C_CONVW + tap * CONV_T + chans[j]), in1=cc[:, q % 4, :],
                                op0=ALU.mult, op1=ALU.add).then_inc(taps, 1)
                    lo_to(u + 2 * i + 4)

                def take_z(i):
                    dve.wait_ge(unit_done, z + 2 * i + 2)
                    if g >= 1:
                        dve.wait_ge(yl_done, GT * g)
                    for j in range(2):
                        dve.tensor_tensor(zs[:, 2 * i + j, :], bank(T[("z", g, i)] + j), rstd[:], ALU.mult
                                          ).then_inc(evac, 1)

                def take_out(g, i):
                    dve.wait_ge(unit_done, U[("out", g)] + i + 1)
                    for j in range(2):
                        if g:
                            dve.wait_ge(evac, T[("out", g - 1, i)] + j + 1)
                        dve.tensor_tensor(h[:, 2 * i + j, :], h[:, 2 * i + j, :], bank(T[("out", g, i)] + j), ALU.add
                                          ).then_inc(evac, 1)

                take_z(0)
                lo_to(z + 3)
                for c in range(SB):
                    take(("xseq", g), c, xseq[:, c, :])
                dve.wait_ge(filled, FILL[("bseq", g)] + 1)
                dve.tensor_copy(bseq[:], bank(T[("bseq", g)]).rearrange("p (c n) -> p c n", c=SB)).then_inc(evac, 1)
                take(("cb", g), 0, cbT[:])
                def spread(ap, hp, d):
                    h0 = HEADS * d + HPG * g + 2 * hp
                    return ap[:, :, h0:h0 + 2].rearrange("p c h -> p h c").unsqueeze(3).to_broadcast([P, 2, SB, P])

                def mask(ap):
                    return ap[:].unsqueeze(1).unsqueeze(1).to_broadcast([P, 2, SB, P])

                def weights(hp):
                    n = GT * g + hp
                    if n >= 1:
                        dve.wait_ge(m_done, n)
                    for dst, d, m in ((wf, 0, le), (wb, 1, ge)):
                        dve.tensor_tensor(dst[:], spread(dt_seq, hp, d), mask(m), ALU.mult).then_inc(w_done, 1)
                    dve.wait_ge(w_done, 3 * n + 2)
                    dve.tensor_tensor(wf[:], wf[:], wb[:], ALU.add).then_inc(w_done, 1)

                def weigh(hp):
                    n = GT * g + hp
                    m = mm[:, n % 2]
                    dve.wait_ge(exp_done, n + 1)
                    dve.tensor_tensor(m, m, cbT[:].unsqueeze(1).to_broadcast([P, 2, SEQ]), ALU.mult).then_inc(m_half, 1)
                    dve.wait_ge(m_half, n + 1)
                    dve.wait_ge(w_done, 3 * n + 3)
                    dve.tensor_tensor(m, m, wf[:].rearrange("p h c l -> p h (c l)"), ALU.mult).then_inc(m_done, 1)

                def finish(hp):
                    n = GT * g + hp
                    dve.wait_ge(y_full, n + 1)
                    dve.scalar_tensor_tensor(out=xT[:, hp, :], in0=xT[:, hp, :], scalar=d_col[:, n:n + 1],
                                             in1=pe_y[:], op0=ALU.mult, op1=ALU.add).then_inc(y_skip, 1)
                    dve.wait_ge(y_skip, n + 1)
                    dve.wait_ge(z_silu, n + 1)
                    dve.tensor_tensor(xT[:, hp, :], xT[:, hp, :], zs[:, hp, :], ALU.mult).then_inc(gated, 1)

                if g == 0:
                    dt_steps()
                    take_z(1)
                    lo_to(z + 5)
                    dt_sums()
                chunks = [(0, 0), (1, SB - 1), (0, 1), (1, SB - 2), (0, 2), (1, SB - 3)]

                def heads(ap):
                    return ap.rearrange("p (h q) -> p h q", h=HPG)

                def per_head(ap):
                    return ap.unsqueeze(2).to_broadcast([P, HPG, HD])

                def hcols(d):
                    return slice(HEADS * d + HPG * g, HEADS * d + HPG * g + HPG)

                def decay_x(n):
                    d, c = chunks[n]
                    dve.wait_ge(evac, T[("xseq", g)] + c + 1)
                    if n >= 2:
                        dve.wait_ge(filled, FILL[("state", g, 0)] + n - 1)
                    dve.tensor_tensor(heads(xd[:, n % 2, :]), heads(xseq[:, c, :]), per_head(epq[:, 1, c, hcols(d)]),
                                      ALU.mult).then_inc(xd_done, 1)

                def after_state(n):
                    return T[("state", g, n // 4 * 4)] + n % 4 + 1

                decay_x(0)
                decay_x(1)
                if g:
                    weights(0)
                    take_z(1)
                    lo_to(z + 5)
                for n in range(6):
                    d, c = chunks[n]
                    if n == 4 and g:
                        take_out(g - 1, 0)
                        lo_to(w + 2)
                    into = c if d == 0 else c - 1
                    if n >= 2:
                        prev = into - 1 if d == 0 else into + 1
                        dve.wait_ge(evac, after_state(n - 2))
                        if n > 2:
                            dve.wait_ge(evac, after_state(n - 1))
                        dve.tensor_tensor(heads(ytmp[:]), heads(car[:, d, prev, :]), per_head(etot[:, c, hcols(d)]),
                                          ALU.mult).then_inc(car_mul, 1)
                        dve.wait_ge(car_mul, 4 * g + n - 1)
                        dve.wait_ge(filled, FILL[("state", g, 0)] + n + 1)
                        dve.tensor_tensor(car[:, d, into, :], ytmp[:], bank(after_state(n) - 1), ALU.add
                                          ).then_inc(evac, 1)
                    else:
                        take(("state", g, 0), n, car[:, d, into, :])
                    if n + 2 < 6:
                        decay_x(n + 2)
                offs = [(0, 1), (1, 2), (0, 2), (1, 1), (0, 3), (1, 0)]
                dve.wait_ge(evac, after_state(5))
                adds = 0
                for n in range(6):
                    d, c = offs[n]
                    second = n in (2, 3)
                    dst = ytmp if second else yo[:, c, :]
                    dve.wait_ge(filled, FILL[("yoff", g)] + n + 1)
                    if second and adds:
                        dve.wait_ge(yo_add, 2 * g + adds)
                    dve.tensor_tensor(heads(dst[:] if second else dst), heads(bank(T[("yoff", g)] + n)),
                                      per_head(epq[:, 0, c, hcols(d)]), ALU.mult).then_inc(evac, 1)
                    if second:
                        dve.wait_ge(evac, T[("yoff", g)] + n + 1)
                        dve.tensor_tensor(yo[:, c, :], yo[:, c, :], ytmp[:], ALU.add).then_inc(yo_add, 1)
                        adds += 1

                if g == 0:
                    weights(0)
                for hp in range(GT):
                    weigh(hp)
                    if g:
                        lo_to(w + hp + 2)
                    if hp:
                        finish(hp - 1)
                    if hp + 1 < GT:
                        weights(hp + 1)
                        if g:
                            take_out(g - 1, hp + 1)
                finish(GT - 1)
                dve.wait_ge(gsq_used, GT * g + GT)
                dve.tensor_scalar(var[:], pe_s[:], 1.0 / GC, EPS, ALU.mult, ALU.add).then_inc(gvar, 1)
                dve.wait_ge(gstd, g + 1)
                dve.reciprocal(ytmp[:], var[:]).then_inc(grstd, 1)
                dve.wait_ge(grstd, g + 1)
                if g < GROUPS - 1:
                    lo_to(U[("xbc", g + 1)] + 2)
                for m in range(GT):
                    dve.wait_ge(gated, GT * g + m + 1)
                    dve.scalar_tensor_tensor(out=zs[:, m, :], in0=xT[:, m, :], scalar=col(C_SSDN + GT * g + m),
                                             in1=ytmp[:], op0=ALU.mult, op1=ALU.mult).then_inc(yn_done, 1)
                for m in range(GT):
                    dve.wait_ge(yh_done, GT * g + m + 1)
                    dve.tensor_tensor(yl[:, m, :], zs[:, m, :], yh[:, m, :].bitcast(F32), ALU.subtract
                                      ).then_inc(yl_done, 1)
            for i in range(4):
                take_out(GROUPS - 1, i)
                lo_to(U[("out", GROUPS - 1)] + i + 2)
                for m in (2 * i, 2 * i + 1):
                    u_lo(1, m, uh0, ul0)

            lr = par[:, C_A:C_A + 2 * J]
            li = par[:, C_A + 2 * J:C_A + 4 * J]
            step, mag, sin, sin_half, n_, ang, lam_r, lam_i, q_r, q_i, cos, s_c, mag4 = (
                v5[:, i, :] for i in range(13))
            s_a, s_b, s_d = ang, step, n_
            count = [0]

            def v(op, *a, **k):
                if count[0]:
                    dve.wait_ge(v_dve, count[0])
                op(*a, **k).then_inc(v_dve, 1)
                count[0] += 1

            def tt(o, a, b, f):
                v(dve.tensor_tensor, o, a, b, f)

            def by_block(a):
                return a.rearrange("p (d b j) -> p d b j", d=2, b=NB)

            def in_blocks(a):
                return a.rearrange("p (b d j) -> p d b j", d=2, b=NB)

            def s5_angles():
                dve.wait_ge(v_act, 1)
                tt(mag, lr, step, ALU.mult)
                tt(ang, li, step, ALU.mult)
                v(dve.tensor_scalar, n_, ang, 1.0 / (2.0 * PI), ROUND_MAGIC, ALU.mult, ALU.add)
                v(dve.tensor_scalar, n_, n_, -ROUND_MAGIC, None, ALU.add)
                for part_ in (TWO_PI_HI, TWO_PI_MID, TWO_PI_LO):
                    v(dve.scalar_tensor_tensor, out=ang, in0=n_, scalar=-part_, in1=ang, op0=ALU.mult,
                      op1=ALU.add)
                v(dve.tensor_scalar, ang, ang, PI_BELOW, -PI_BELOW, ALU.min, ALU.max)

            def s5_lambda_q():
                dve.wait_ge(v_act, 4)
                tt(sin_half, sin_half, sin_half, ALU.mult)
                v(dve.tensor_scalar, cos, sin_half, -2.0, 1.0, ALU.mult, ALU.add)
                tt(lam_r, mag, cos, ALU.mult)
                tt(lam_i, mag, sin, ALU.mult)
                v(dve.tensor_scalar, s_a, lam_r, -1.0, None, ALU.add)
                tt(s_b, lr, lr, ALU.mult)
                tt(s_c, li, li, ALU.mult)
                tt(s_b, s_b, s_c, ALU.add)
                v(dve.reciprocal, s_b, s_b)
                tt(s_c, s_a, lr, ALU.mult)
                tt(s_d, lam_i, li, ALU.mult)
                tt(s_c, s_c, s_d, ALU.add)
                tt(q_r, s_c, s_b, ALU.mult)
                tt(s_c, lam_i, lr, ALU.mult)
                tt(s_d, s_a, li, ALU.mult)
                tt(s_c, s_c, s_d, ALU.subtract)
                tt(q_i, s_c, s_b, ALU.mult)

            def s5_phases():
                tt(s_a, mag, mag, ALU.mult)
                tt(mag4, s_a, s_a, ALU.mult)
                tt(s_a, cos, cos, ALU.mult)
                tt(s_b, sin, sin, ALU.mult)
                v(dve.scalar_tensor_tensor, out=s_c, in0=cos, scalar=2.0, in1=sin, op0=ALU.mult, op1=ALU.mult)
                tt(s_d, s_a, s_b, ALU.subtract)
                tt(s_a, s_d, s_d, ALU.mult)
                tt(s_b, s_c, s_c, ALU.mult)
                tt(cos, s_a, s_b, ALU.subtract)
                v(dve.scalar_tensor_tensor, out=sin, in0=s_c, scalar=2.0, in1=s_d, op0=ALU.mult, op1=ALU.mult)

                for d, sign in ((0, 1.0), (1, -1.0)):
                    v(dve.tensor_copy, in_blocks(tn[:, 0, 0, :])[:, d], by_block(cos)[:, d])
                    v(dve.tensor_scalar, in_blocks(tn[:, 1, 0, :])[:, d], by_block(sin)[:, d], sign, None, ALU.mult)
                    v(dve.tensor_copy, in_blocks(m4v[:])[:, d], by_block(mag4)[:, d])
                    for kind in range(2):
                        for a, lam in ((0, lam_r), (1, lam_i)):
                            v(dve.tensor_copy, lamx[:, a, :, (2 * kind + d) * BP:(2 * kind + d + 1) * BP],
                              by_block(lam)[:, d])

            def s5_turns():
                for n in range(1, 7):
                    tt(s_a, tn[:, 0, n - 1, :], tn[:, 0, n - 1, :], ALU.mult)
                    tt(s_b, tn[:, 1, n - 1, :], tn[:, 1, n - 1, :], ALU.mult)
                    tt(tn[:, 0, n, :], s_a, s_b, ALU.subtract)
                    v(dve.scalar_tensor_tensor, out=tn[:, 1, n, :], in0=tn[:, 0, n - 1, :], scalar=2.0,
                      in1=tn[:, 1, n - 1, :], op0=ALU.mult, op1=ALU.mult)

            def s5_take_c():
                for n in range(8):
                    dve.wait_ge(filled, FILL["c5"] + n + 1)
                    src = bank(T["c5"] + n).rearrange("p (b j g q) -> p b j g q", b=4, j=BP, g=2)
                    for g in range(2):
                        rows = slice(64 * g, 64 * g + 64)
                        dve.tensor_copy(cst[rows, n // 2, 4 * (n % 2):4 * (n % 2) + 4, :, :],
                                        src[rows, :, :, g, :]).then_inc((c5_half, evac)[g], 1)

            prod = [t[:].rearrange("p (a x) k -> p a (x k)", a=2).rearrange(
                "p a (j q) -> p a j q", q=S5H) for t in (ta, tb)]
            c_all = cst.rearrange("p (a d) b j q -> p d a (b j) q", a=2)

            def s5_c_q(d):
                dve.wait_ge(evac, T["c5"] + 8)
                dve.wait_ge(c5_half, 8)
                for a in range(2):
                    for pr_, qv in ((prod[0], q_r), (prod[1], q_i)):
                        tt(pr_[:, a], c_all[:, d, a],
                           qv[:, d * J:(d + 1) * J].unsqueeze(2).to_broadcast([P, J, S5H]), ALU.mult)
                tt(cw[:, 0, d], prod[0][:, 0], prod[1][:, 1], ALU.subtract)
                tt(cw[:, 1, d], prod[0][:, 1], prod[1][:, 0], ALU.add)

            for layer in range(2):
                gh, gl, p_in, ph, pl, pproj = FFN[layer]
                if layer == 1:
                    v(dve.memset, rot[:, 0, :, 0:1], 1.0)
                    v(dve.memset, rot[:, 1, :, 0:1], 0.0)
                    dve.wait_ge(v_dve, count[0])
                    dve.drain().then_inc(cw_done, 1)

                    dirs = "p (d j) k -> p d (j k)"
                    t0, f0 = T["s5"], FILL["s5"]
                    e_re, e_im = ring[:, (t0 + 4) % 4:(t0 + 4) % 4 + 2, :], ring[:, (t0 + 6) % 4:(t0 + 6) % 4 + 2, :]
                    c_, s_ = (rot[:, a].rearrange(dirs, d=2) for a in range(2))
                    z_ = [zz[:, a].rearrange(dirs, d=2) for a in range(2)]
                    a_, b_ = ta[:].rearrange(dirs, d=2), tb[:].rearrange(dirs, d=2)
                    m_ = m4[:].rearrange(dirs, d=2)
                    def powers(b):
                        dve.wait_ge(pw0, b * 8 + 8)
                        lam = [lamx[:, a, bass.ds(b, 1), :].rearrange("p b q -> p (b q)").unsqueeze(1).unsqueeze(3)
                               .to_broadcast([P, 2, 4 * BP, S5H]) for a in range(2)]
                        for tau in range(TAU):
                            now = pw[:, tau].rearrange("p a q j h -> p a (q j) h")
                            then = pw[:, tau + 1].rearrange("p a q j h -> p a (q j) h")
                            if tau:
                                dve.wait_ge(pw_r, b * (2 * TAU) + 2 * tau)
                            q = slice(0, 4 * BP if tau < TAU - 1 else 2 * BP)
                            x, y = px[:, :, q], py[:, :, q]
                            dve.tensor_tensor(x, now[:, :, q], lam[0][:, :, q], ALU.mult).then_inc(pw_x, 1)
                            dve.tensor_tensor(y, now[:, :, q], lam[1][:, :, q], ALU.mult).then_inc(pw_x, 1)
                            dve.wait_ge(pw_x, b * (2 * TAU) + 2 * tau + 2)
                            dve.tensor_tensor(then[:, 0, q], x[:, 0], y[:, 1], ALU.subtract).then_inc(pw_r, 1)
                            dve.tensor_tensor(then[:, 1, q], x[:, 1], y[:, 0], ALU.add).then_inc(pw_r, 1)

                    def rotations(b):
                        for n in range(7):
                            w = 1 << n
                            turn = [tn[:, a, n, bass.ds(b * 8, 8)].unsqueeze(1).unsqueeze(3)
                                    .to_broadcast([P, 2, 2 * BP, w]) for a in range(2)]
                            tx = [t[:].rearrange("p (a x) k -> p a (x k)", a=2)[:, :, 0:2 * BP * w].rearrange(
                                "p a (q k) -> p a q k", k=w) for t in (ta, tb)]
                            if n:
                                dve.wait_ge(rot_r, b * 14 + 2 * n)
                            for x_, tr in zip(tx, turn):
                                dve.tensor_tensor(x_, rot[:, :, :, 0:w], tr, ALU.mult).then_inc(rot_x, 1)
                            dve.wait_ge(rot_x, b * 14 + 2 * n + 2)
                            dve.tensor_tensor(rot[:, 0, :, w:2 * w], tx[0][:, 0], tx[1][:, 1], ALU.subtract
                                              ).then_inc(rot_r, 1)
                            dve.tensor_tensor(rot[:, 1, :, w:2 * w], tx[0][:, 1], tx[1][:, 0], ALU.add
                                              ).then_inc(rot_r, 1)

                    def drives(b):
                        dve.wait_ge(filled, b * 8 + (f0 + 8))
                        dve.wait_ge(rot_r, b * 14 + 14)
                        dve.tensor_tensor(a_, e_re, c_, ALU.mult).then_inc(spin, 1)
                        dve.tensor_tensor(b_, e_im, s_, ALU.mult).then_inc(spin, 1)
                        dve.wait_ge(spin, b * 5 + 2)
                        dve.tensor_tensor(z_[0], a_, b_, ALU.add).then_inc(spin, 1)
                        dve.wait_ge(spin, b * 5 + 3)
                        dve.tensor_tensor(a_, e_im, c_, ALU.mult).then_inc(spin, 1)
                        dve.tensor_tensor(b_, e_re, s_, ALU.mult).then_inc(evac, 4)
                        dve.wait_ge(spin, b * 5 + 4)
                        dve.wait_ge(evac, b * 8 + (t0 + 8))
                        dve.tensor_tensor(z_[1], a_, b_, ALU.subtract).then_inc(spin, 1)

                    def states(b):
                        dve.wait_ge(spin, b * 5 + 5)
                        dve.wait_ge(m4_r, b * 8 + 8)
                        for z1, o1 in zip(z_, (a_, b_)):
                            for d in range(2):
                                r = slice(None, None, (1, -1)[d])
                                dve.tensor_tensor_scan(o1[:, d][:, r], m_[:, d][:, r], z1[:, d][:, r], 0.0,
                                                       ALU.mult, ALU.add).then_inc(scan, 1)
                        dve.wait_ge(scan, b * 4 + 4)
                        dve.wait_ge(y5_full, b + 2)
                        kk = "p (j k) -> p j k"
                        for q, (f, g) in enumerate(((a_, c_), (b_, s_), (b_, c_), (a_, s_))):
                            for d in range(2):
                                o = xs[:, q, d, :, 1 - d:1 - d + NCH]
                                f1, g1 = f[:, d].rearrange(kk, j=BP), g[:, d].rearrange(kk, j=BP)
                                if q == 1:
                                    dve.scalar_tensor_tensor(out=o, in0=f1, scalar=-1.0, in1=g1, op0=ALU.mult,
                                                             op1=ALU.mult).then_inc(xs_r, 1)
                                else:
                                    dve.tensor_tensor(o, f1, g1, ALU.mult).then_inc(xs_r, 1)
                        dve.wait_ge(xs_r, b * 8 + 8)

                    powers(0)
                    rstd_of(3)
                    for m in range(KD):
                        dve.scalar_tensor_tensor(out=u5[:, m, :], in0=h[:, m, :], scalar=col(NORM_COL[3] + m),
                                                 in1=rstd[:], op0=ALU.mult, op1=ALU.mult).then_inc(u5_done, 1)
                    rotations(0)
                    with dve.Fori(0, NB - 1) as b:
                        powers(b + 1)
                        drives(b)
                        states(b)
                        rotations(b + 1)
                    drives(NB - 1)
                    states(NB - 1)
                    for m in range(KD):
                        dve.wait_ge(g5_hi, m + 1)
                        dve.tensor_tensor(gl5[:, m, :], u5[:, m, :], gh5[:, m, :].bitcast(F32), ALU.subtract
                                          ).then_inc(g5_lo, 1)
                    u, t = U["glu"], T["glu"]
                    for i in range(4):
                        for half in range(2):
                            lo_to(u + 4 * i + 2 * half + 2)
                            dve.wait_ge(unit_done, u + 4 * i + 2 * half + 2)
                            if i:
                                dve.wait_ge(h_upd, KD + 2 * i)
                            for j in range(2):
                                dve.tensor_scalar(cc[:, 2 * half + j, :], bank(t + 4 * i + 2 * half + j),
                                                  col(C_BGLU + half * KD + 2 * i + j), None, ALU.add
                                                  ).then_inc(evac, 1)
                            lo_to(u + 4 * i + 2 * half + 3)
                        for j in range(2):
                            dve.wait_ge(glu_sig, 2 * i + j + 1)
                            dve.tensor_tensor(cc[:, j, :], cc[:, j, :], cc[:, 2 + j, :], ALU.mult).then_inc(glu_mul, 1)
                        for j in range(2):
                            dve.wait_ge(glu_mul, 2 * i + j + 1)
                            dve.tensor_tensor(h[:, 2 * i + j, :], h[:, 2 * i + j, :], cc[:, j, :], ALU.add
                                              ).then_inc(h_upd, 1)
                        for m in (2 * i, 2 * i + 1):
                            u_lo(4, m, uh1, ul1)
                rstd_of(1 + 3 * layer)
                u, t = U[("up", layer)], T[("up", layer)]
                lo_to(u + 2)
                done = layer * HT
                with dve.Fori(0, PAIRS) as i:
                    for half in range(2):
                        dve.wait_ge(unit_done, i * 4 + (u + 2 * half + 2))
                        dve.wait_ge(f_taps, i * 8 + (4 * done + 4 * half + 1))
                        for j in range(2):
                            dve.tensor_tensor(cin[:, j, 2:2 + SEQ], bank(t + 2 * half + j), rstd[:], ALU.mult
                                              ).then_inc(evac, 1)
                        lo(u + 2 * half + 3, at=i * 4)
                        for tap in range(1, 3):
                            for j in range(2):
                                if tap == 1:
                                    dve.wait_ge(f_c0, i * 4 + (2 * done + 2 * half + j + 1))
                                else:
                                    dve.wait_ge(f_taps, i * 8 + (4 * done + 4 * half + j + 2))
                                c = 2 * HT * (3 * layer + tap) + half * HT + j
                                dve.scalar_tensor_tensor(out=cc[:, 2 * half + j, :], in0=cin[:, j, 1 + tap:1 + tap + SEQ],
                                                         scalar=dcol(i * 2 + (C_FCW + c)), in1=cc[:, 2 * half + j, :],
                                                         op0=ALU.mult, op1=ALU.add).then_inc(f_taps, 1)
                        if half == 0:
                            lo(u + 4, at=i * 4)
                    for j in range(2):
                        dve.wait_ge(f_silu, i * 2 + (done + j + 1))
                        dve.wait_ge(f_taps, i * 8 + (4 * done + 6 + j + 2))
                        dve.tensor_tensor(cc[:, 2 + j, :], cc[:, j, :], cc[:, 2 + j, :], ALU.mult).then_inc(f_gv, 1)
                    lo(u + 6, at=i * 4)
                    for j in range(2):
                        dve.wait_ge(f_gh, i * 2 + (done + j + 1))
                        dve.tensor_tensor(gl[:, bass.ds(i * 2 + j, 1), :].rearrange("p a t -> p (a t)"), cc[:, 2 + j, :],
                                          gh[:, bass.ds(i * 2 + j, 1), :].rearrange("p a t -> p (a t)").bitcast(F32),
                                          ALU.subtract).then_inc(f_gl, 1)
                split[0] = U[("down", layer)] + 2
                dve.wait_ge(f_gv, HT * (layer + 1) + 2)
                for k in range(PK):
                    take(("p", layer), k, cc[:, k, :])
                for k in range(PK):
                    dve.wait_ge(p_hi, PK * layer + k + 1)
                    dve.tensor_tensor(pl[:, k, :], cc[:, k, :], ph[:, k, :].bitcast(F32), ALU.subtract).then_inc(p_lo, 1)
                u, t = U[("down", layer)], T[("down", layer)]
                r = 2 + 3 * layer
                for i in range(4):
                    lo_to(u + 6 * i + 6)
                    dve.wait_ge(unit_done, u + 6 * i + 6)
                    for m in (2 * i, 2 * i + 1):
                        dve.tensor_tensor(h[:, m, :], h[:, m, :], bank(t + m), ALU.add).then_inc(evac, 1)
                    lo_to(u + 6 * i + 7)
                    for m in (2 * i, 2 * i + 1):
                        u_lo(r, m, UH[layer], UL[layer])
                    if layer == 0:
                        (s5_angles, s5_lambda_q, s5_phases, s5_turns)[i]()
                for i in range(2):
                    if i:
                        rstd_of(r)
                    lo_to(U[("proj", layer)] + i + 1)
                    dve.wait_ge(unit_done, U[("proj", layer)] + i + 1)
                    for m in range(4 * i, 4 * i + 4):
                        dve.tensor_copy(pproj[:, m, :], bank(T[("proj", layer)] + m)).then_inc(evac, 1)
                    lo_to(U[("proj", layer)] + i + 2)
                u = U[("gate", layer)]
                before = 2 * KD * layer
                for i in range(4):
                    lo_to(u + 2 * i + 2)
                    dve.wait_ge(unit_done, u + 2 * i + 2)
                    if i >= 2:
                        dve.wait_ge(h_upd, before + 2 * i - 2)
                    if i == 0:
                        dve.wait_ge(p_lo, PK * (layer + 1))
                    for m in (2 * i, 2 * i + 1):
                        dve.tensor_tensor(cc[:, m % 4, :], bank(T[("gate", layer, m // 4)] + m % 4), rstd[:], ALU.mult
                                          ).then_inc(evac, 1)
                    lo_to(u + 2 * i + 3)
                    for m in (2 * i, 2 * i + 1):
                        dve.wait_ge(g_sig, KD * layer + m + 1)
                        dve.tensor_tensor(cc[:, m % 4, :], cc[:, m % 4, :], pproj[:, m, :], ALU.mult).then_inc(g_mul, 1)
                    if layer == 0 and i == 1:
                        s5_take_c()
                    lo_to(min(u + 2 * i + 4, u + 9))
                    for m in (2 * i, 2 * i + 1):
                        dve.wait_ge(g_mul, KD * layer + m + 1)
                        dve.tensor_tensor(h[:, m, :], h[:, m, :], cc[:, m % 4, :], ALU.add).then_inc(h_upd, 1)
                    if layer == 0 and i >= 2:
                        s5_c_q(i - 2)

            rstd_of(6)
            for m in range(KD):
                dve.wait_ge(*h_ready(6, m))
                dve.scalar_tensor_tensor(out=hn[:, m, :], in0=h[:, m, :], scalar=col(NORM_COL[6] + m), in1=rstd[:],
                                         op0=ALU.mult, op1=ALU.mult).then_inc(hn_done, 1)
            for b in range(SB):
                for half in range(2):
                    take("final", 2 * b + half, o_sb[:, b, half * SEQ:(half + 1) * SEQ])

        @block.tensor
        def _(pe):
            def product(u, t, nk, k0, rh, rl, at=0, tiles=2, width=P, first=True, last=True):
                pe.wait_ge(lo_done, at + (u + 1))
                if first:
                    pe.wait_ge(evac, at + (t + tiles - 4))
                wh, wl = part(w_hi, u, nk), part(w_lo, u, nk)
                for j in range(tiles):
                    o = bank(t + j)[0:width, :]
                    for k in range(nk):
                        c = slice(j * width, j * width + width)
                        pe.matmul(o, wh[:, k, c], rh[:, k0 + k, :], start=first and k == 0, stop=False)
                        pe.matmul(o, wh[:, k, c], rl[:, k0 + k, :], start=False, stop=False)
                        mm_ = pe.matmul(o, wl[:, k, c], rh[:, k0 + k, :], start=False, stop=last and k == nk - 1)
                mm_.then_inc(unit_done, 1)

            def add_square(r, m):
                pe.wait_ge(sq_done, KD * r + m + 1)
                if m == 0 and r == 1:
                    pe.wait_ge(gvar, GROUPS)
                elif m == 0 and r > 1:
                    pe.wait_ge(var_done, r)
                pe.matmul(pe_s[:], ones[:], sq[:, m % 2, :], start=m == 0, stop=m == KD - 1).then_inc(sq_used, 1)

            pe.wait_ge(masks, 11)
            pe.wait_ge(in_par, 16 * 16)
            pe.wait_ge(step_x, 1)
            for i in range(7):
                mm_ = pe.transpose(bank(T["params"] + i // 4)[:, (i % 4) * P:(i % 4 + 1) * P], stage[:, i, :], eye[:])
                if i in (3, 6):
                    mm_.then_inc(filled, 1)
            pe.wait_ge(in_x, 16)
            for m in range(KD):
                if T["x"] + m >= 4:
                    pe.wait_ge(evac, T["x"] + m - 3)
                for b in range(SB):
                    mm_ = pe.transpose(bank(T["x"] + m)[:, b * P:(b + 1) * P], x_in[:, b, m * P:(m + 1) * P], eye[:])
                mm_.then_inc(filled, 1)
                if m:
                    add_square(0, m - 1)
            add_square(0, KD - 1)
            pe.wait_ge(ul_done, KD)
            product(U["dt"], T["dt"], KD, 0, uh0, ul0, tiles=1, width=2 * HEADS)

            def dt_sums():
                pe.wait_ge(evac, T["seq"] - 3)
                pe.wait_ge(adt, 1)
                s_t = bank(T["seq"]).rearrange("p (a c q) -> p a c q", a=2, c=SB)
                for a, src in enumerate((dtT, adT)):
                    for c in range(SB):
                        mm_ = pe.transpose(s_t[:, a, c, :], src[:, c * P:(c + 1) * P], eye[0:2 * HEADS, 0:2 * HEADS])
                mm_.then_inc(filled, 1)
                pe.wait_ge(evac, T["sums"])
                s_t = bank(T["sums"]).rearrange("p (a c q) -> p a c q", a=2, c=SB)
                for a, d, m in ((0, 0, le), (0, 1, ge), (1, 0, gt), (1, 1, lt)):
                    q = slice(HEADS * d, HEADS * d + HEADS)
                    mm_ = pe.matmul(s_t[:, a, :, q], m[:], ad_seq[:, :, q], start=True, stop=True)
                mm_.then_inc(filled, 1)
                pe.wait_ge(evac, T["totals"] - 3)
                pe.matmul(bank(T["totals"])[:, 0:SB * 2 * HEADS], ones[:], ad_seq[:].rearrange("p c q -> p (c q)"),
                          start=True, stop=True).then_inc(filled, 1)

            for g in range(GROUPS):
                def group_square(g, hp):
                    n = GT * g + hp
                    pe.wait_ge(gsq, n + 1)
                    if hp == 0:
                        pe.wait_ge(*((gvar, g) if g else (var_done, 1)))
                    pe.matmul(pe_s[:], ones[:], sq[:, n % 2, :], start=hp == 0, stop=hp == GT - 1).then_inc(gsq_used, 1)

                def exponents(hp):
                    n = GT * g + hp
                    pe.wait_ge(r_done, 16 * n + 16)
                    if n:
                        pe.wait_ge(exp_done, n)
                    for k in range(2):
                        pe.matmul(pe_e[:, k, :], gt[:], rr[:, 0, k].rearrange("p c l -> p (c l)"), start=True, stop=False)
                        mm_ = pe.matmul(pe_e[:, k, :], lt[:], rr[:, 1, k].rearrange("p c l -> p (c l)"), start=False,
                                        stop=True)
                    mm_.then_inc(e_full, 1)

                def z_product(i):
                    for kg in range(2):
                        product(U[("z", g)] + 2 * i + kg, T[("z", g, i)], 4, 4 * kg, uh0, ul0, first=kg == 0,
                                last=kg == 1)

                def out_product(g, i):
                    product(U[("out", g)] + i, T[("out", g, i)], GT, 0, yh, yl)

                u = U[("xbc", g)]
                for i in range(3):
                    for kg in range(2):
                        product(u + 2 * i + kg, T[("xbc", g)] + 2 * i, 4, 4 * kg, uh0, ul0, first=kg == 0, last=kg == 1)
                        if g and (i, kg) == (0, 0):
                            group_square(g - 1, GT - 1)
                z_product(0)
                pe.wait_ge(silu, 6 * g + 6)
                for c in range(SB):
                    ck = slice(c * P, c * P + P)
                    pe.wait_ge(evac, T[("xseq", g)] + c - 3)
                    for i in range(GT):
                        mm_ = pe.transpose(bank(T[("xseq", g)] + c)[:, i * P:(i + 1) * P], xT[:, i, ck], eye[:])
                    mm_.then_inc(filled, 1)
                pe.wait_ge(evac, T[("bseq", g)] - 3)
                for c in range(SB):
                    ck = slice(c * P, c * P + P)
                    mm_ = pe.transpose(bank(T[("bseq", g)])[:, ck], bT[:, ck], eye[:])
                mm_.then_inc(filled, 1)
                pe.wait_ge(evac, T[("cb", g)] - 3)
                for c in range(SB):
                    ck = slice(c * P, c * P + P)
                    mm_ = pe.matmul(bank(T[("cb", g)])[:, ck], bT[:, ck], cT[:, ck], start=True, stop=True)
                mm_.then_inc(filled, 1)
                z_product(1)
                if g:
                    exponents(0)
                else:
                    dt_sums()
                pe.wait_ge(evac, T[("bseq", g)] + 1)
                for n, (d, c) in enumerate([(0, 0), (1, SB - 1), (0, 1), (1, SB - 2), (0, 2), (1, SB - 3)]):
                    t = T[("state", g, n // 4 * 4)] + n % 4
                    if n == 4:
                        if g:
                            pe.wait_ge(yl_done, GT * g)
                            out_product(g - 1, 0)
                        else:
                            exponents(0)
                    pe.wait_ge(xd_done, 6 * g + n + 1)
                    pe.wait_ge(evac, t - 3)
                    pe.matmul(bank(t), bseq[:, c, :], xd[:, n % 2, :], start=True, stop=True
                              ).then_inc(filled, 1)
                exponents(1)
                for n, (d, c) in enumerate([(0, 1), (1, 2), (0, 2), (1, 1), (0, 3), (1, 0)]):
                    pe.wait_ge(evac, max(T[("state", g, n // 4 * 4)] + n % 4 + 1, T[("yoff", g)] + n - 3))
                    pe.matmul(bank(T[("yoff", g)] + n), cT[:, c * P:(c + 1) * P], car[:, d, c - 1 if d == 0 else c, :],
                              start=True, stop=True).then_inc(filled, 1)

                def outputs(hp):
                    n = GT * g + hp
                    if n:
                        pe.wait_ge(y_skip, n)
                    if hp == 0:
                        pe.wait_ge(evac, T[("yoff", g)] + 6)
                        pe.wait_ge(yo_add, 2 * g + 2)
                    for c in range(SB):
                        pe.matmul(pe_y[:, c * P:(c + 1) * P], yo[:, c, hp * P:(hp + 1) * P], eye[:], start=c == 0,
                                  stop=False, skip_group_check=True)
                    pe.wait_ge(m_done, n + 1)
                    for k in range(2):
                        for c in range(SB):
                            mm_ = pe.matmul(pe_y[64 * k:64 * k + 64, c * P:(c + 1) * P],
                                            xseq[:, c, (2 * hp + k) * HD:(2 * hp + k + 1) * HD],
                                            mm[:, n % 2, k, c * P:(c + 1) * P], start=False,
                                            stop=True, skip_group_check=True)
                    mm_.then_inc(y_full, 1)

                for hp in range(GT):
                    if hp + 1 < GT and g:
                        out_product(g - 1, hp + 1)
                    outputs(hp)
                    if hp + 2 < GT:
                        exponents(hp + 2)
                    if hp:
                        group_square(g, hp - 1)
            group_square(GROUPS - 1, GT - 1)
            pe.wait_ge(yl_done, GT * GROUPS)
            for i in range(4):
                out_product(GROUPS - 1, i)
                if i:
                    add_square(1, 2 * i - 2)
                    add_square(1, 2 * i - 1)

            for layer in range(2):
                gh, gl, p_in, ph, pl, pproj = FFN[layer]
                uh, ul = UH[layer], UL[layer]
                r = 1 + 3 * layer
                if layer == 1:
                    pe.sem_inc(y5_full, 2)
                    t0 = T["s5"]

                    def tables(b, slot):
                        pe.wait_ge(blk, b * 16 + 17)
                        for n in range(4):
                            pe.wait_ge(evac, b * 8 + (t0 + n - 3))
                            for j in range(BP):
                                mm_ = pe.transpose(bank(t0 + n)[:, j * P:(j + 1) * P],
                                                   vblk[:, n // 2, n % 2, j].rearrange("p t q -> p (t q)"), eye[:])
                            mm_.then_inc(filled, 1)
                        pe.wait_ge(k_evac, b + 1)
                        for j in range(BP):
                            for s in range(TAU):
                                o = pe_e[CH * s:CH * s + CH, 0, j * P:(j + 1) * P]
                                for d in range(2):
                                    for a in range(2):
                                        b_in = vblk[:, a, 1, j, 0, :]
                                        if d == 0:
                                            c_out, oo = cblk[slot][:, a, 0, j, 0:TAU - s, :], o[:, CH * s:]
                                        else:
                                            c_out, oo = cblk[slot][:, a, 1, j, TAU - s:TAU + 1, :], o[:, 0:CH * (s + 1)]
                                        mm_ = pe.matmul(oo, b_in, c_out.rearrange("p t q -> p (t q)"),
                                                        start=(j, d, a) == (0, 0, 0), stop=False,
                                                        skip_group_check=True)
                        pe.wait_ge(d_diag, b * BP + BP)
                        for j in range(BP):
                            mm_ = pe.matmul(pe_e[:, 0, j * P:(j + 1) * P], eye[:], ddiag[:, j, :], start=False,
                                            stop=j == BP - 1, skip_group_check=True)
                        mm_.then_inc(k_full, 1)
                        pe.wait_ge(lift, b * 16 + 16)
                        for n in range(4):
                            pe.wait_ge(evac, b * 8 + (t0 + n + 1))
                            for j in range(BP):
                                mm_ = pe.matmul(bank(t0 + 4 + n)[:, j * P:(j + 1) * P], vT[:, n // 2, n % 2, j, :],
                                                ulift[slot][:, j, :], start=True, stop=True)
                            mm_.then_inc(filled, 1)

                    def outputs5(b, slot):
                        pe.wait_ge(k_evac, b + 2)
                        pe.wait_ge(xs_r, b * 8 + 8)
                        pe.wait_ge(y5_gelu, b * 16 + 1)
                        for j in range(BP):
                            o = pe_y[:, j * NCH:(j + 1) * NCH]
                            pe.matmul(o, kT[:, j, :], ulift[slot][:, j, :], start=j == 0, stop=False, skip_group_check=True)
                            for q in range(4):
                                pe.matmul(o, cblk[slot][:, q // 2, 0, j, 1:TAU + 1, :].rearrange("p t q -> p (t q)"),
                                          xs[:, q, 0, j, 0:NCH], start=False, stop=False, skip_group_check=True)
                                mm_ = pe.matmul(o, cblk[slot][:, q // 2, 1, j, 0:TAU, :].rearrange("p t q -> p (t q)"),
                                                xs[:, q, 1, j, 1:NCH + 1], start=False, stop=q == 3,
                                                skip_group_check=True)
                        mm_.then_inc(y5_full, 1)

                    tables(0, 0)
                    with pe.Fori(0, NB // 2 - 1) as i:
                        for slot in range(2):
                            tables(i * 2 + (slot + 1), 1 - slot)
                            outputs5(i * 2 + slot, slot)
                    tables(NB - 1, 1)
                    outputs5(NB - 2, 0)
                    outputs5(NB - 1, 1)
                    u, t = U["glu"], T["glu"]
                    for i in range(4):
                        for half in range(2):
                            for kg in range(2):
                                if i == 0 and half == 0:
                                    pe.wait_ge(g5_lo, 4 * kg + 4)
                                product(u + 4 * i + 2 * half + kg, t + 4 * i + 2 * half, 4, 4 * kg, gh5, gl5,
                                        first=kg == 0, last=kg == 1)
                        if i:
                            add_square(4, 2 * i - 2)
                            add_square(4, 2 * i - 1)
                add_square(r, KD - 2)
                add_square(r, KD - 1)
                u, t = U[("up", layer)], T[("up", layer)]
                with pe.Fori(0, PAIRS) as i:
                    for half in range(2):
                        for kg in range(2):
                            if half == 0:
                                pe.wait_ge(ul_done, KD * SPLIT[r] + 4 * kg + 4)
                            product(u + 2 * half + kg, t + 2 * half, 4, 4 * kg, uh, ul, at=i * 4, first=kg == 0,
                                    last=kg == 1)
                pe.wait_ge(p_loaded[layer], 16)
                for k in range(PK):
                    pe.wait_ge(evac, T[("p", layer)] + k - 3)
                    for b in range(SB):
                        mm_ = pe.transpose(bank(T[("p", layer)] + k)[:, b * P:(b + 1) * P],
                                           p_in[:, b, k * P:(k + 1) * P], eye[:])
                    mm_.then_inc(filled, 1)
                u, t = U[("down", layer)], T[("down", layer)]
                for i in range(4):
                    for kg in range(6):
                        nk = min(4, HT - 4 * kg)
                        if i == 0:
                            pe.wait_ge(f_gl, HT * layer + 4 * kg + nk + 2)
                        product(u + 6 * i + kg, t + 2 * i, nk, 4 * kg, gh, gl, first=kg == 0, last=kg == 5)
                    if i:
                        add_square(r + 1, 2 * i - 2)
                        add_square(r + 1, 2 * i - 1)
                pe.wait_ge(p_lo, PK * (layer + 1))
                for i in range(2):
                    product(U[("proj", layer)] + i, T[("proj", layer)] + 4 * i, PK, 0, ph, pl, tiles=4)
                    if i == 0:
                        add_square(r + 1, KD - 2)
                        add_square(r + 1, KD - 1)
                pe.wait_ge(ul_done, KD * SPLIT[r + 1] + KD)
                u = U[("gate", layer)]
                for i in range(4):
                    for kg in range(2):
                        product(u + 2 * i + kg, T[("gate", layer, i // 2)] + i % 2 * 2, 4, 4 * kg, uh, ul,
                                first=kg == 0, last=kg == 1)
                    if layer == 0 and i == 1:
                        pe.wait_ge(c_loaded, 16 * 8)
                        for n in range(8):
                            pe.wait_ge(evac, T["c5"] + n - 3)
                            for k in range(4):
                                mm_ = pe.transpose(bank(T["c5"] + n)[:, k * P:(k + 1) * P],
                                                   c_in[:, n // 2, 4 * (n % 2) + k, :], eye[:])
                            mm_.then_inc(filled, 1)
                    if i:
                        add_square(r + 2, 2 * i - 2)
                        add_square(r + 2, 2 * i - 1)
                add_square(r + 2, KD - 2)
                add_square(r + 2, KD - 1)

            for b in range(SB):
                for half in range(2):
                    if b == 0:
                        pe.wait_ge(hn_done, 4 * half + 4)
                    pe.wait_ge(evac, T["final"] + 2 * b + half - 3)
                    for k in range(4):
                        mm_ = pe.transpose(bank(T["final"] + 2 * b + half)[:, k * P:(k + 1) * P],
                                           hn[:, 4 * half + k, b * P:(b + 1) * P], eye[:])
                    mm_.then_inc(filled, 1)


_INS = ['x', 'p', 'ssd_w_in', 'ssd_conv_w', 'ssd_conv_b', 'ssd_dt_bias', 'ssd_a_log', 'ssd_d', 'ssd_norm_w',
        'ssd_w_out', 's5_a_re', 's5_a_im', 's5_log_step', 's5_b_re', 's5_b_im', 's5_c_re', 's5_c_im', 's5_d',
        's5_w_glu', 's5_b_glu', 'mix_norm_w', 'ffn_norm_w', 'ffn_w_up', 'ffn_conv_w', 'ffn_conv_b', 'ffn_w_down',
        'ple_norm_w', 'ple_w_gate', 'ple_w_proj', 'final_norm_w']


def kernel(**inputs):
    import numpy as _np
    import concourse.bacc as _bacc
    from concourse import mybir as _mybir
    from concourse.bass_utils import run_bass_kernel_spmd as _run

    nc = _bacc.Bacc("TRN2", target_bir_lowering=False, num_devices=1)
    arrays, args = {}, {}
    for name in _INS:
        a = _np.ascontiguousarray(inputs[name])
        arrays[f"in_{name}"] = a
        args[name] = nc.dram_tensor(f"in_{name}", a.shape, _mybir.dt.from_np(a.dtype), kind="ExternalInput").ap()
    out = nc.dram_tensor("out_0", inputs["x"].shape, _mybir.dt.float32, kind="ExternalOutput").ap()
    bidir_hybrid_kernel(nc, args, out)
    r = _run(nc, [arrays], core_ids=[0])
    return r.results[0]["out_0"]
```
